# Optimizing a Trainium2 kernel written in Bass

```python
import math
import jax, jax.numpy as jnp
from jax import lax
import numpy as np

D_MODEL = 4096
BATCH = 1
SEQ = 256
DEPTH = 1

D_MIX = D_MODEL
W_CONV = D_MIX // 2
CONV_GROUPS = 16
CONV_K = 3
N_HEADS = 16
HEAD_DIM = (D_MIX - W_CONV) // N_HEADS
N_KV = 4
GQA = N_HEADS // N_KV
W_ATT = N_HEADS * HEAD_DIM
W_KV = N_KV * HEAD_DIM
L_CMP = 32
D_CMP = 16
L_SLC = 64
N_SEL = 16
N_LOCAL = 2
WIN = 512
Q_BLOCK = 128
SEL_Q_CHUNK = 32
N_BRANCH = 3
DEEPNORM_ALPHA = (2 * DEPTH) ** 0.25
DEEPNORM_BETA = (8 * DEPTH) ** -0.25
LN_EPS = 1e-5
NEG = -1e30
BIG = 1e9

SPLIT_SIZES = (W_CONV, W_CONV, W_CONV, W_CONV,
               W_ATT,
               W_KV, W_KV, W_KV, W_KV, W_KV, W_KV,
               W_ATT,
               N_HEADS * N_BRANCH)
N_IN = sum(SPLIT_SIZES)

kernel_name = "hymba_conv_nsa_deepnorm"

def layer_norm(x, g, b):
    x32 = x.astype(jnp.float32)
    mu = x32.mean(-1, keepdims=True)
    var = jnp.square(x32 - mu).mean(-1, keepdims=True)
    y = (x32 - mu) * lax.rsqrt(var + LN_EPS) * g.astype(jnp.float32) + b.astype(jnp.float32)
    return y.astype(x.dtype)

def short_conv_mixer(h, bg, cg, w):
    u = cg * h
    y = lax.conv_general_dilated(u, w[:, None, :].astype(u.dtype), window_strides=(1,),
                                 padding=[(CONV_K - 1, 0)],
                                 dimension_numbers=('NWC', 'WIO', 'NWC'),
                                 feature_group_count=W_CONV)
    return bg * y

def compress_blocks(kv, pos, w1, w2):
    b, t, g, d = kv.shape
    n_chunk = t // D_CMP
    r = L_CMP // D_CMP
    n_cmp = n_chunk - r + 1
    chunks = kv.reshape(b, n_chunk, D_CMP, g, d)
    blocks = jnp.concatenate([chunks[:, i:i + n_cmp] for i in range(r)], axis=2)
    blocks = blocks + pos[None, None, :, None, :]
    flat = blocks.transpose(0, 1, 3, 2, 4).reshape(b, n_cmp, g, L_CMP * d)
    hid = jax.nn.silu(jnp.einsum('bngf,fe->bnge', flat, w1))
    return jnp.einsum('bnge,ed->bngd', hid, w2)

def band_slabs(x):
    b, t, g, d = x.shape
    n_qb = t // Q_BLOCK
    n_wb = WIN // Q_BLOCK
    xp = jnp.pad(x, ((0, 0), (WIN, 0), (0, 0), (0, 0))).reshape(b, n_qb + n_wb, Q_BLOCK, g, d)
    return jnp.concatenate([xp[:, i:i + n_qb] for i in range(n_wb + 1)], axis=2)

def nsa_mixer(q, k_cmp, v_cmp, k_slc, v_slc, k_win, v_win, gate_logits,
              pos_k, w1_k, w2_k, pos_v, w1_v, w2_v):
    b, t, _ = q.shape
    scale = 1.0 / math.sqrt(HEAD_DIM)
    f32 = jnp.float32
    q5 = q.reshape(b, t, N_KV, GQA, HEAD_DIM)
    kv4 = lambda a: a.reshape(b, t, N_KV, HEAD_DIM)
    tpos = jnp.arange(t)

    kc = compress_blocks(kv4(k_cmp), pos_k, w1_k, w2_k)
    vc = compress_blocks(kv4(v_cmp), pos_v, w1_v, w2_v)
    n_cmp = kc.shape[1]
    cmp_end = jnp.arange(n_cmp) * D_CMP + L_CMP - 1
    cmp_valid = cmp_end[None, :] <= tpos[:, None]
    s = jnp.einsum('btgrd,bngd->bgrtn', q5, kc).astype(f32) * scale
    p_cmp = jax.nn.softmax(jnp.where(cmp_valid, s, NEG), axis=-1) * cmp_valid
    o_cmp = jnp.einsum('bgrtn,bngd->btgrd', p_cmp.astype(vc.dtype), vc)

    n_slc = t // L_SLC
    ci = jnp.arange(n_cmp)[:, None]
    sj = jnp.arange(n_slc)[None, :]
    overlap = ((ci * D_CMP < (sj + 1) * L_SLC) & (ci * D_CMP + L_CMP > sj * L_SLC)).astype(f32)
    p_slc = jnp.einsum('bgrtn,nj->bgtj', p_cmp, overlap)
    cur = tpos // L_SLC
    jj = jnp.arange(n_slc)
    block_valid = jj[None, :] <= cur[:, None]
    forced = (jj == 0)[None, :] | (block_valid & (jj[None, :] > cur[:, None] - N_LOCAL))
    sel_score = jnp.where(forced, BIG, jnp.where(block_valid, p_slc, -1.0))
    n_sel = min(N_SEL, n_slc)
    _, sel_idx = lax.top_k(sel_score, n_sel)

    kb = kv4(k_slc).reshape(b, n_slc, L_SLC, N_KV, HEAD_DIM).transpose(0, 3, 1, 2, 4)
    vb = kv4(v_slc).reshape(b, n_slc, L_SLC, N_KV, HEAD_DIM).transpose(0, 3, 1, 2, 4)
    bi = jnp.arange(b)[:, None, None, None]
    gi = jnp.arange(N_KV)[None, :, None, None]
    n_ch = t // SEL_Q_CHUNK
    q_ch = q5.reshape(b, n_ch, SEL_Q_CHUNK, N_KV, GQA, HEAD_DIM).transpose(1, 0, 2, 3, 4, 5)
    i_ch = sel_idx.reshape(b, N_KV, n_ch, SEL_Q_CHUNK, n_sel).transpose(2, 0, 1, 3, 4)
    t_ch = tpos.reshape(n_ch, SEL_Q_CHUNK)

    def sel_chunk(args):
        qc, ic, tc = args
        kg = kb[bi, gi, ic]
        vg = vb[bi, gi, ic]
        kpos = ic[..., None] * L_SLC + jnp.arange(L_SLC)
        mask = kpos <= tc[None, None, :, None, None]
        sc = jnp.einsum('bqgrd,bgqnld->bgrqnl', qc, kg).astype(f32) * scale
        sc = jnp.where(mask[:, :, None], sc, NEG).reshape(b, N_KV, GQA, SEL_Q_CHUNK, n_sel * L_SLC)
        pc = jax.nn.softmax(sc, axis=-1).astype(vg.dtype)
        return jnp.einsum('bgrqk,bgqkd->bqgrd', pc,
                          vg.reshape(b, N_KV, SEL_Q_CHUNK, n_sel * L_SLC, HEAD_DIM))

    o_slc = lax.map(sel_chunk, (q_ch, i_ch, t_ch))
    o_slc = o_slc.transpose(1, 0, 2, 3, 4, 5).reshape(b, t, N_KV, GQA, HEAD_DIM)

    n_qb = t // Q_BLOCK
    kw = band_slabs(kv4(k_win))
    vw = band_slabs(kv4(v_win))
    qb = q5.reshape(b, n_qb, Q_BLOCK, N_KV, GQA, HEAD_DIM)
    n_key = WIN + Q_BLOCK
    qpos = jnp.arange(n_qb)[:, None, None] * Q_BLOCK + jnp.arange(Q_BLOCK)[None, :, None]
    kpos = jnp.arange(n_qb)[:, None, None] * Q_BLOCK - WIN + jnp.arange(n_key)[None, None, :]
    wmask = (kpos <= qpos) & (kpos > qpos - WIN) & (kpos >= 0)
    sw = jnp.einsum('bnqgrd,bnkgd->bngrqk', qb, kw).astype(f32) * scale
    pw = jax.nn.softmax(jnp.where(wmask[None, :, None, None], sw, NEG), axis=-1).astype(vw.dtype)
    o_win = jnp.einsum('bngrqk,bnkgd->bnqgrd', pw, vw).reshape(b, t, N_KV, GQA, HEAD_DIM)

    gates = jax.nn.sigmoid(gate_logits.reshape(b, t, N_KV, GQA, N_BRANCH))
    o = gates[..., 0:1] * o_cmp + gates[..., 1:2] * o_slc + gates[..., 2:3] * o_win
    return o.reshape(b, t, W_ATT)

def hybrid_layer(x, w_in, conv_w, pos_k, w1_k, w2_k, pos_v, w1_v, w2_v, w_out, ln_g, ln_b):
    proj = jnp.einsum('btd,df->btf', x, w_in)
    split_at = [int(v) for v in np.cumsum(SPLIT_SIZES)[:-1]]
    (h, bg, cg, z_conv, q, k_cmp, v_cmp, k_slc, v_slc, k_win, v_win,
     z_att, gate_logits) = jnp.split(proj, split_at, axis=-1)
    y_conv = short_conv_mixer(h, bg, cg, conv_w) * jax.nn.silu(z_conv)
    y_att = nsa_mixer(q, k_cmp, v_cmp, k_slc, v_slc, k_win, v_win, gate_logits,
                      pos_k, w1_k, w2_k, pos_v, w1_v, w2_v) * jax.nn.silu(z_att)
    mixed = jnp.concatenate([y_conv, y_att], axis=-1)
    out = jnp.einsum('btf,fd->btd', mixed, w_out)
    return layer_norm(DEEPNORM_ALPHA * x + out, ln_g, ln_b)

def setup_inputs(seed: int = 0) -> dict:
    key = jax.random.key(seed)
    ks = jax.random.split(key, 12)
    f32 = jnp.float32

    def nrm(k, shape, s):
        return jax.random.normal(k, shape, f32) * s

    return {
        "x": nrm(ks[0], (BATCH, SEQ, D_MODEL), 1.0),
        "w_in": nrm(ks[1], (DEPTH, D_MODEL, N_IN), D_MODEL ** -0.5),
        "conv_w": nrm(ks[2], (DEPTH, CONV_K, W_CONV), CONV_K ** -0.5),
        "cmp_pos_k": nrm(ks[3], (DEPTH, L_CMP, HEAD_DIM), 0.2),
        "cmp_w1_k": nrm(ks[4], (DEPTH, L_CMP * HEAD_DIM, HEAD_DIM), (L_CMP * HEAD_DIM) ** -0.5),
        "cmp_w2_k": nrm(ks[5], (DEPTH, HEAD_DIM, HEAD_DIM), HEAD_DIM ** -0.5),
        "cmp_pos_v": nrm(ks[6], (DEPTH, L_CMP, HEAD_DIM), 0.2),
        "cmp_w1_v": nrm(ks[7], (DEPTH, L_CMP * HEAD_DIM, HEAD_DIM), (L_CMP * HEAD_DIM) ** -0.5),
        "cmp_w2_v": nrm(ks[8], (DEPTH, HEAD_DIM, HEAD_DIM), HEAD_DIM ** -0.5),
        "w_out": nrm(ks[9], (DEPTH, D_MIX, D_MODEL), D_MIX ** -0.5 * DEEPNORM_BETA),
        "ln_g": 1.0 + nrm(ks[10], (DEPTH, D_MODEL), 0.02),
        "ln_b": nrm(ks[11], (DEPTH, D_MODEL), 0.02),
    }

def reference(x, w_in, conv_w, cmp_pos_k, cmp_w1_k, cmp_w2_k, cmp_pos_v, cmp_w1_v, cmp_w2_v,
              w_out, ln_g, ln_b):
    for l in range(DEPTH):
        x = hybrid_layer(x, w_in[l], conv_w[l], cmp_pos_k[l], cmp_w1_k[l], cmp_w2_k[l],
                         cmp_pos_v[l], cmp_w1_v[l], cmp_w2_v[l], w_out[l], ln_g[l], ln_b[l])
    return x


_drawn_inputs = setup_inputs


def setup_inputs(seed=0):
    import zlib

    import numpy as np

    out = dict(_drawn_inputs(seed))
    spreads = {}
    factors = {'cmp_pos_k': 8.0,
     'cmp_w1_k': 5.151,
     'cmp_w2_k': 5.103,
     'cmp_pos_v': 5.001,
     'ln_g': 2.853,
     'ln_b': 2.87}
    for name, (base, spread) in spreads.items():
        noise = np.random.default_rng([zlib.crc32(name.encode()), seed]).standard_normal(out[name].shape)
        drawn = base * np.exp(spread * noise) if base else spread * noise
        out[name] = __import__('jax').numpy.asarray(drawn.astype(out[name].dtype))
    for name, factor in factors.items():
        out[name] = (out[name] * factor).astype(out[name].dtype)
    return out
```

```python
from contextlib import ExitStack

import numpy as np

import concourse.bass as bass
from concourse import mybir

F32 = mybir.dt.float32
F32R = mybir.dt.float32r
BF16 = mybir.dt.bfloat16
ALU = mybir.AluOpType
ACT = mybir.ActivationFunctionType
AX = mybir.AxisListType

P = 128
D = 4096
T = 256
TT = T // P
KT = D // P
W = 512
WC = 2048
HD = 128
NKV = 4
GQA = 4
WKV = NKV * HD
LC, DC = 32, 16
NC = T // DC - LC // DC + 1
SCALE = float(HD) ** -0.5
ALPHA = 2.0 ** 0.25
EPS = 1e-5
NEG = -1e30

C_H, C_BG, C_CG, C_ZC, C_Q = (WC * i for i in range(5))
C_KCMP = 5 * WC
C_VCMP = C_KCMP + WKV
C_KV = C_VCMP + WKV
C_ZA = C_KV + 4 * WKV
C_GATE = C_ZA + WC
NG = 48

GK = 2
GC = KT // GK
RING = 4
AHEAD = RING - 1
PRO = 2 * GC + 2 + 8
CH = 7
TURN = CH * GC
OUT0 = PRO + NKV * TURN
NOUT = D // W
LAST = OUT0 + NOUT * GC
assert TURN % RING == 0 and GC % RING == 0

ZA, KV, Q, H, CG, ZC, BG = range(CH)
PAIR = (1, 0, 1, 0, 1, 0, 2)
I_CMP, I_S, I_T, I_V, PERIOD = 54, 56, 60, 63, 10
I_U = CH * GC - 14
COLS = {ZA: C_ZA, Q: C_Q, H: C_H, CG: C_CG, ZC: C_ZC, BG: C_BG}


FW = 1024
FIN = T // P * D // FW
FIN_POOL = (1, 4)
FIN_DVE = tuple(i for i in range(FIN) if i not in FIN_POOL)


class Signal:

    def __init__(self, sem, per=0, before=0):
        self.sem, self.per, self.before = sem, per, before

    def at(self, g, k):
        return g * self.per + (self.before + k)


def chunk_done(g, c):
    return g * TURN + (PRO + GC * (c + 1))


def landed_at(n, g=0, per=TURN):
    first, twice = PRO + KV * GC, GC // RING
    if n >= OUT0:
        extra, again = NKV * twice, 0
    else:
        extra, again = min(max((n - first) // RING + 1, 0), twice), twice
    return g * (16 * (per // RING + again)) + 16 * (n // RING + 1 + extra)


def over_keys(m):
    return m[:, :, :].rearrange("p r (t a) -> p (r t) a", a=1).to_broadcast([P, GQA * TT, NC])


def build(nc, x, w_in, conv_w, pos_k, w1_k, w2_k, pos_v, w1_v, w2_v, w_out, ln_g, ln_b, out):
    x, out = x[0], out[0]
    w_in, conv_w, w_out = w_in[0], conv_w[0], w_out[0]
    pos, w1, w2 = (pos_k[0], pos_v[0]), (w1_k[0], w1_v[0]), (w2_k[0], w2_v[0])

    with ExitStack() as ctx:
        top = [(nc.sbuf_base + 31) // 32 * 32]

        def region(kib):
            at = top[0]
            top[0] += int(kib * 1024)
            return at

        def place(name, shape, dt, at):
            return nc.alloc_sbuf_tensor_at(name, shape, dt, offset=at)

        def own(name, shape, dt):
            size = int(np.prod(shape[1:])) * (2 if dt == BF16 else 4)
            return place(name, shape, dt, region((size + 31) // 32 * 32 / 1024))

        r_x = region(64)
        xt_hi = place("xt_hi", [P, KT, T], F32R, r_x)
        xt_lo = place("xt_lo", [P, KT, T], F32R, r_x + 32 * 1024)
        y = place("y", [P, TT, D], F32, r_x)
        gamma = place("gamma", [P, D], F32, r_x + 32 * 1024)
        beta = place("beta", [P, D], F32, r_x + 48 * 1024)

        r_m = region(64)
        mix_hi = place("mix_hi", [P, KT, T], F32R, r_m)
        mix_lo = place("mix_lo", [P, KT, T], F32R, r_m + 32 * 1024)
        x_tok = place("x_tok", [P, TT, D], F32, r_m)
        a_tok = place("a_tok", [P, 2, 2, TT, W], F32, r_m)
        a_hi = place("a_hi", [P, 2, 2, NKV, T], F32R, r_m + 32 * 1024)
        a_lo = place("a_lo", [P, 2, 2, NKV, T], F32R, r_m + 48 * 1024)

        raw = [own(f"raw{i}", [P, GK * W], F32) for i in range(RING)]
        w_hi = [own(f"w_hi{i}", [P, GK * W], F32R) for i in range(RING)]
        w_lo = [own(f"w_lo{i}", [P, GK * W], F32R) for i in range(RING)]

        r_s = top[0]
        tok_a = own("tok_a", [P, TT, W], F32)
        tok_b = own("tok_b", [P, TT, W], F32)
        k_t = own("k_t", [P, 2, T], F32)
        q_t = own("q_t", [P, GQA, T], F32)
        z_t = own("z_t", [P, GQA, T], F32)
        r_prob = top[0]
        prob = own("prob", [P, TT, 2, T], F32)
        p_t0 = own("p_t0", [P, 2, T], F32)
        p_t1 = own("p_t1", [P, 2, P], F32)
        pc_t = own("pc_t", [P, T], F32)
        conv = place("conv", [P, 4, T], F32, r_prob)
        att = own("att", [P, T], F32)
        ident = own("ident", [P, P], F32)
        ident_b = own("ident_b", [P, P], BF16)
        causal = own("causal", [P, P], BF16)
        c_neg = own("c_neg", [P, TT, NC], F32)
        c_ok = own("c_ok", [P, TT, NC], F32)
        taps = own("taps", [P, 3, 16], F32)
        taps_g = own("taps_g", [P, 3, 4], F32)
        gates = own("gates", [P, TT, NG], F32)
        gates_g = own("gates_g", [P, TT, GQA * 3], F32)
        kc = own("kc", [P, NKV, NC], F32)
        kc_g = own("kc_g", [P, NC], F32)
        vc = own("vc", [P, NKV, HD], F32)
        vc_g = own("vc_g", [P, HD], F32)
        sc = own("sc", [P, GQA, TT, NC], F32)
        ec = own("ec", [P, GQA, TT, NC], F32)
        c_max = own("c_max", [P, GQA, TT], F32)
        c_sum = own("c_sum", [P, GQA, TT], F32)
        c_rcp = own("c_rcp", [P, GQA, TT], F32)
        c_fac = own("c_fac", [P, GQA, TT], F32)
        s_max = own("s_max", [P, TT, 2], F32)
        s_neg = own("s_neg", [P, TT, 2], F32)
        s_sum = own("s_sum", [P, TT, 2], F32)
        s_rcp = own("s_rcp", [P, TT, 2], F32)
        s_fac = own("s_fac", [P, TT, 2], F32)
        assert top[0] <= nc.sbuf_usable_end, (top[0], nc.sbuf_usable_end)

        conv_rows = place("conv_rows", [48, P], F32, r_s + 8 * 1024)
        pos_sb = place("pos_sb", [P, 2, 2, HD], F32, r_s + 9 * 1024)
        w2_sb = place("w2_sb", [P, 2, HD], F32, r_s + 11 * 1024)
        hid = place("hid", [P, 2, NC, NKV], F32, r_s + 12 * 1024)
        x_res = [place(f"x_res{i}", [P, TT, W], F32, r_s + 4096 * i) for i in range(2)]
        stats = place("stats", [P, TT, NOUT, 6], F32, r_s + 8192)
        mv = place("mv", [P, TT, 2], F32, r_s + 9 * 1024)
        eps = place("eps", [P, 1], F32, r_s + 9 * 1024 + 64)
        std = place("std", [P, TT], F32, r_s + 9 * 1024 + 128)
        rstd = place("rstd", [P, TT], F32, r_s + 9 * 1024 + 192)
        shift = place("shift", [P, TT], F32, r_s + 9 * 1024 + 256)

        bank = [ctx.enter_context(nc.psum_tensor(f"bank{i}", [P, W], F32)) for i in range(8)]

        def sem(name):
            return ctx.enter_context(nc.semaphore(name))

        landed = [sem(f"landed{i}") for i in range(RING)]
        s_hi = sem("s_hi")
        s_lo = sem("s_lo")
        s_used = sem("s_used")
        s_const = sem("s_const")
        s_pool = sem("s_pool")
        s_small = sem("s_small")
        x_in = [sem(f"x_in{i}") for i in range(4)]
        xt_ps, xt_h, xt_l = sem("xt_ps"), sem("xt_h"), sem("xt_l")
        taps_ps, taps_in = sem("taps_ps"), sem("taps_in")
        a_in = sem("a_in")
        a_ps, a_h, a_l = sem("a_ps"), sem("a_h"), sem("a_l")
        gates_in = sem("gates_in")
        hid_in = sem("hid_in")
        c_ps, c_in = sem("c_ps"), sem("c_in")

        group_in = Signal(sem("group_in"), 4)
        g_tok = Signal(sem("g_tok"), 2)
        g_ps = Signal(sem("g_ps"), 2)
        y_in = Signal(sem("y_in"), 2)
        y_hi = Signal(sem("y_hi"), 2)
        y_lo = Signal(sem("y_lo"), 2)
        za_tok = Signal(sem("za_tok"), 2)
        z_ps = Signal(sem("z_ps"), 2)
        z_in = Signal(sem("z_in"), 2)
        kv_tok = Signal(sem("kv_tok"), 2)
        k_ps = Signal(sem("k_ps"), 1)
        k_in = Signal(sem("k_in"), 1)
        q_tok = Signal(sem("q_tok"), 2)
        q_ps = Signal(sem("q_ps"), 2)
        q_in = Signal(sem("q_in"), 2)
        sc_ps = Signal(sem("sc_ps"), 1)
        sc_v = Signal(sem("sc_v"), 3)
        ec_in = Signal(sem("ec_in"), 1)
        pc_v = Signal(sem("pc_v"), 5)
        s_ps = Signal(sem("s_ps"), 2 * GQA)
        mx_v = Signal(sem("mx_v"), 2 * GQA)
        neg_v = Signal(sem("neg_v"), GQA)
        exp_in = Signal(sem("exp_in"), GQA)
        rcp_v = Signal(sem("rcp_v"), 2 * GQA)
        p_in = Signal(sem("p_in"), 2 * GQA)
        p_ps = Signal(sem("p_ps"), 2 * GQA)
        pt_a = Signal(sem("pt_a"), 2 * GQA)
        pt_v = Signal(sem("pt_v"), 2 * GQA)
        o_ps = Signal(sem("o_ps"), GQA)
        o_in = Signal(sem("o_in"), GQA)
        o_hi = Signal(sem("o_hi"), GQA)
        o_lo = Signal(sem("o_lo"), GQA)
        h_tok = Signal(sem("h_tok"), 2)
        u_tok = Signal(sem("u_tok"), 2)
        zc_tok = Signal(sem("zc_tok"), 2, 2)
        u_ps = Signal(sem("u_ps"), 2)
        cv = Signal(sem("cv"), 12, 1)

        res_in = [sem(f"res_in{i}") for i in range(2)]
        norm_in = sem("norm_in")
        y_sum = sem("y_sum")
        y_stat = sem("y_stat")
        mv_in, std_in = sem("mv_in"), sem("std_in")
        rstd_in, shift_in = sem("rstd_in"), sem("shift_in")
        n_scaled, n_gamma = sem("n_scaled"), sem("n_gamma")
        n_out_v, n_out_p = sem("n_out_v"), sem("n_out_p")
        stored = sem("stored")
        small = 16 * (1 + 2 * (P // DC + 1))

        block = ctx.enter_context(nc.Block())

        def as_f32(ap):
            return ap.bitcast(F32)

        @block.sync
        def _(sp):
            def load(slot, src, shape):
                k, c = shape
                dst = raw[slot][:, 0:k * c].rearrange("p (k c) -> p k c", k=k)
                sp.dma_start(dst, src).then_inc(landed[slot], 16)

            def rows(w, r0, n, c0, width):
                return w[bass.ds(r0, n * P), bass.ds(c0, width)].rearrange("(k p) c -> p k c", p=P)

            n = 0
            for q in range(4):
                cols = slice(q * D // 4, (q + 1) * D // 4)
                sp.dma_start(x_tok[:, :, cols], x[:, cols].rearrange("(t p) c -> p t c", p=P)
                             ).then_inc(x_in[q], 16)
                if n < RING:
                    for _ in range(2):
                        load(n % RING, rows(w_in, n * GK * P, GK, C_KCMP, W), (GK, W))
                        n += 1
            for n in range(RING, 2 * GC):
                sp.wait_ge(s_lo, n - AHEAD)
                c0 = C_KCMP if n < GC else C_VCMP
                load(n % RING, rows(w_in, n % GC * GK * P, GK, c0, W), (GK, W))
            for j in range(2):
                n = 2 * GC + j
                sp.wait_ge(s_lo, n - AHEAD)
                load(n % RING, rows(w_in, j * 16 * P, 16, C_GATE, NG), (16, NG))
            for j in range(8):
                n = 2 * GC + 2 + j
                sp.wait_ge(s_lo, n - AHEAD)
                load(n % RING, rows(w1[j // 4], j % 4 * 8 * HD, 8, 0, HD), (8, HD))

            with sp.Fori(0, NKV) as g:
                for c in range(CH):
                    with sp.Fori(0, GC // RING) as j:
                        for k in range(RING):
                            n = PRO + c * GC + k
                            sp.wait_ge(s_lo, g * TURN + j * RING + (n - AHEAD))
                            r0 = j * (RING * GK * P) + k * GK * P
                            if c == KV:
                                strips = w_in[:, C_KV:C_KV + 4 * WKV].rearrange("r (s c) -> r s c", s=4)
                                for kk in range(GK):
                                    sp.dma_start(
                                        raw[n % RING][:, kk * W:(kk + 1) * W].rearrange(
                                            "p (s c) -> p s c", s=4),
                                        strips[bass.ds(r0 + kk * P, P), :, bass.ds(g * HD, HD)]
                                    ).then_inc(landed[n % RING], 16)
                            else:
                                load(n % RING, rows(w_in, r0, GK, g * W + COLS[c], W), (GK, W))

            with sp.Fori(0, NOUT) as c:
                for half in range(2):
                    with sp.Fori(0, GC // RING // 2) as j:
                        for k in range(RING):
                            n = OUT0 + half * GC // 2 + k
                            sp.wait_ge(s_lo, c * GC + j * RING + (n - AHEAD))
                            r0 = j * (RING * GK * P) + ((1 - half) * WC + k * GK * P)
                            load(n % RING, rows(w_out, r0, GK, c * W, W), (GK, W))

            for i in range(FIN):
                t, c0 = divmod(i * FW, D)
                if i in FIN_POOL:
                    sp.wait_ge(n_out_p, FIN_POOL.index(i) + 1)
                else:
                    sp.wait_ge(n_out_v, FIN_DVE.index(i) + 1)
                sp.dma_start(out[t * P:(t + 1) * P, c0:c0 + FW], y[:, t, c0:c0 + FW]).then_inc(stored, 16)
            sp.wait_ge(stored, 16 * FIN)

        @block.gpsimd
        def _(pool):
            pool.dma_start(conv_rows[:, :], conv_w.rearrange("k (b c) -> (k b) c", c=P)
                           ).then_inc(s_small, 16)
            for i in range(2):
                for a in range(P // DC):
                    pool.dma_start(pos_sb[a * DC:(a + 1) * DC, i],
                                   pos[i].rearrange("(h b) d -> b h d", h=2)).then_inc(s_small, 16)
                pool.dma_start(w2_sb[:, i], w2[i]).then_inc(s_small, 16)
            pool.memset(ident[:, :], 0.0).then_inc(s_pool, 1)
            pool.memset(causal[:, :], 0.0).then_inc(s_pool, 1)
            pool.memset(c_neg[:, :, :], 0.0).then_inc(s_pool, 1)
            pool.memset(c_ok[:, :, :], 1.0).then_inc(s_pool, 1)
            pool.wait_ge(s_pool, 4)
            pool.affine_select(out=ident[:, :], in_=ident[:, :], compare_op=ALU.not_equal, fill=1.0,
                               base=0, pattern=[[-1, P]], channel_multiplier=1).then_inc(s_const, 1)
            pool.affine_select(out=causal[:, :], in_=causal[:, :], compare_op=ALU.is_ge, fill=NEG,
                               base=0, pattern=[[-1, P]], channel_multiplier=1).then_inc(s_const, 1)
            for m, fill in ((c_neg, NEG), (c_ok, 0.0)):
                pool.affine_select(out=m[:, :, :], in_=m[:, :, :], compare_op=ALU.is_ge, fill=fill,
                                   base=-(LC - 1), pattern=[[P, TT], [-DC, NC]],
                                   channel_multiplier=1).then_inc(s_const, 1)
            pool.wait_ge(s_const, 4)
            pool.tensor_copy(ident_b[:, :], ident[:, :]).then_inc(s_const, 1)

            pool.wait_ge(c_in, 2)
            pool.wait_ge(gates_in, 2)
            pool.wait_ge(taps_in, 1)
            with pool.Fori(0, NKV) as g:
                pool.wait_ge(cv.sem, cv.at(g, 0))
                for dst, src in ((kc_g[:, :], kc[:, bass.ds(g, 1), :]),
                                 (vc_g[0:NC, :], vc[0:NC, bass.ds(g, 1), :])):
                    pool.tensor_copy(dst, src.rearrange("p a n -> p (a n)")).then_inc(group_in.sem, 1)
                pool.tensor_copy(taps_g[:, :, :], taps[:, :, bass.ds(g * 4, 4)]).then_inc(group_in.sem, 1)
                pool.tensor_copy(gates_g[:, :, :], gates[:, :, bass.ds(g * (3 * GQA), 3 * GQA)]
                                 ).then_inc(group_in.sem, 1)

            pool.wait_ge(s_used, OUT0)
            for dst, src in ((gamma, ln_g), (beta, ln_b)):
                pool.dma_start(dst[:, :], src.to_broadcast([P, D])).then_inc(norm_in, 16)
            with pool.Fori(0, NOUT // 2) as c2:
                for b in range(2):
                    pool.wait_ge(y_sum, c2 * 4 + (2 * b + 2))
                    pool.dma_start(x_res[b][:, :, :],
                                   x[:, bass.ds(c2 * (2 * W) + b * W, W)].rearrange(
                                       "(t p) c -> p t c", p=P)).then_inc(res_in[b], 16)

            for i in FIN_POOL:
                t, c0 = divmod(i * FW, D)
                pool.wait_ge(n_gamma, i + 1)
                v = y[:, t, c0:c0 + FW]
                pool.tensor_tensor(v, v, beta[:, c0:c0 + FW], ALU.add).then_inc(n_out_p, 1)

        @block.scalar
        def _(act):
            def split(n, g=0, per=TURN):
                s = n % RING
                act.wait_ge(landed[s], landed_at(n, g, per))
                if n >= RING:
                    act.wait_ge(s_used, g * per + (n - AHEAD))
                act.activation(w_hi[s][:, :], raw[s][:, :], ACT.Copy).then_inc(s_hi, 1)

            def split_small(n, width):
                s = n % RING
                act.wait_ge(landed[s], landed_at(n))
                act.wait_ge(s_used, n - AHEAD)
                act.activation(w_hi[s][:, 0:width], raw[s][:, 0:width], ACT.Copy).then_inc(s_hi, 1)

            def x_high(q):
                for b in range(4):
                    act.wait_ge(xt_ps, 4 * q + b + 1)
                    k = 8 * q + 2 * b
                    act.activation(xt_hi[:, k:k + 2, :], bank[4 + b][:, :].rearrange(
                        "p (k t) -> p k t", k=2), ACT.Copy).then_inc(xt_h, 1)

            def a_high(i):
                for b in range(4):
                    act.wait_ge(a_ps, 4 * i + b + 1)
                    h, g0 = b // 2, b % 2 * 2
                    act.activation(a_hi[:, i, h, g0:g0 + 2, :], bank[4 + b][:, :].rearrange(
                        "p (g t) -> p g t", g=2), ACT.Copy).then_inc(a_h, 1)

            x_high(0)
            for n in range(AHEAD):
                split(n)
            for i in range(2 * GC + 10):
                n = i + AHEAD
                if i < GC and i % 4 == 2 and i < GC - 2:
                    x_high(i // 4 + 1)
                if i == GC + 4:
                    a_high(0)
                if i == 2 * GC + 2:
                    for t in range(TT):
                        act.wait_ge(s_used, 2 * GC + 2)
                        act.activation(gates[:, t, :], bank[t][:, 0:NG], ACT.Sigmoid
                                       ).then_inc(gates_in, 1)
                    a_high(1)
                if n < 2 * GC:
                    split(n)
                elif n < 2 * GC + 2:
                    split_small(n, 16 * NG)
                elif n < PRO:
                    split_small(n, 8 * HD)
            for i in range(2):
                act.wait_ge(s_used, 2 * GC + 2 + 4 * (i + 1))
                act.activation(hid[:, i].rearrange("p n g -> p (n g)"), bank[2 + i][:, 0:NC * NKV],
                               ACT.Silu).then_inc(hid_in, 1)
            for n in range(PRO, PRO + AHEAD):
                split(n)

            def evacuate(dst, func, c, g, done):
                act.wait_ge(s_used, chunk_done(g, c))
                for t in range(TT):
                    act.activation(dst[:, t, :], bank[2 * PAIR[c] + t][:, :], func
                                   ).then_inc(done.sem, 1)

            with act.Fori(0, NKV) as g:
                for i in range(TURN):
                    if i == 3:
                        for b in range(2):
                            act.wait_ge(y_in.sem, y_in.at(g, b + 1))
                            act.activation(mix_hi[:, bass.ds(g * 4 + (12 + 2 * b), 2), :],
                                           conv[:, 2 * b:2 * b + 2, :], ACT.Copy).then_inc(y_hi.sem, 1)
                    if i == GC * (ZA + 1):
                        evacuate(tok_a, ACT.Silu, ZA, g, za_tok)
                    if i == GC * (ZA + 1) + 3:
                        act.wait_ge(z_ps.sem, z_ps.at(g, 1))
                        act.activation(z_t[:, 0:2, :], bank[6][:, :].rearrange("p (r t) -> p r t", r=2),
                                       ACT.Copy).then_inc(z_in.sem, 1)
                    if i == GC * (KV + 1):
                        evacuate(tok_b, ACT.Copy, KV, g, kv_tok)
                    if i == GC * (Q + 1):
                        evacuate(tok_a, ACT.Copy, Q, g, q_tok)
                    if i == GC * (Q + 1) + 3:
                        act.wait_ge(q_ps.sem, q_ps.at(g, 1))
                        act.activation(q_t[:, 0:2, :], bank[6][:, :].rearrange("p (r t) -> p r t", r=2),
                                       ACT.Copy).then_inc(q_in.sem, 1)
                    if i == I_CMP + 1:
                        act.wait_ge(sc_v.sem, sc_v.at(g, 3))
                        act.activation(ec[:, :, :, :], sc[:, :, :, :], ACT.Exp, scale=SCALE
                                       ).then_inc(ec_in.sem, 1)
                    for r in range(GQA):
                        if i == I_S + PERIOD * r:
                            act.wait_ge(neg_v.sem, neg_v.at(g, r + 1))
                            for t in range(TT):
                                for b in range(2):
                                    keys = (t + 1) * P
                                    last = act.activation(
                                        prob[:, t, b, 0:keys], bank[4 + t][:, b * keys:(b + 1) * keys],
                                        ACT.Exp, scale=SCALE, bias=s_neg[:, t, b:b + 1],
                                        accum_out=s_sum[:, t, b:b + 1])
                            last.then_inc(exp_in.sem, 1)
                        if i == I_T + PERIOD * r:
                            act.wait_ge(p_ps.sem, p_ps.at(g, 2 * r + 1))
                            act.activation(p_t0[:, :, 0:P], bank[6][:, 0:2 * P].rearrange(
                                "p (b q) -> p b q", b=2), ACT.Copy).then_inc(pt_a.sem, 1)
                            act.activation(pc_t[0:NC, :], bank[6][0:NC, 2 * P:4 * P], ACT.Copy
                                           ).then_inc(pt_a.sem, 1)
                        if i == I_V + PERIOD * r:
                            act.wait_ge(o_in.sem, o_in.at(g, r + 1))
                            act.activation(mix_hi[:, bass.ds(g * 4 + r, 1), :].rearrange("p a t -> p (a t)"),
                                           att[:, :], ACT.Copy).then_inc(o_hi.sem, 1)
                    if i == GC * (H + 1):
                        evacuate(tok_a, ACT.Copy, H, g, h_tok)
                    if i == GC * (ZC + 1):
                        evacuate(tok_b, ACT.Silu, ZC, g, zc_tok)
                    split(PRO + i + AHEAD, g)

            for b in range(2):
                act.wait_ge(y_in.sem, y_in.at(NKV, b + 1))
                act.activation(mix_hi[:, KT - 4 + 2 * b:KT - 2 + 2 * b, :], conv[:, 2 * b:2 * b + 2, :],
                               ACT.Copy).then_inc(y_hi.sem, 1)
            with act.Fori(0, NOUT - 1) as c:
                for i in range(GC):
                    split(OUT0 + i + AHEAD, c, GC)
            for i in range(GC - AHEAD):
                split(OUT0 + (NOUT - 1) * GC + i + AHEAD)

            act.wait_ge(mv_in, 2)
            act.activation(std[:, :], mv[:, :, 1], ACT.Sqrt, bias=eps[:, :]).then_inc(std_in, 1)
            act.wait_ge(shift_in, 1)
            for i in range(FIN):
                t, c0 = divmod(i * FW, D)
                v = y[:, t, c0:c0 + FW]
                act.activation(v, v, ACT.Identity, scale=rstd[:, t:t + 1], bias=shift[:, t:t + 1]
                               ).then_inc(n_scaled, 1)

        @block.vector
        def _(dve):
            def split(n, g=0, per=TURN, width=GK * W):
                s = n % RING
                dve.wait_ge(s_hi, g * per + (n + 1))
                dve.tensor_tensor(w_lo[s][:, 0:width], raw[s][:, 0:width], as_f32(w_hi[s][:, 0:width]),
                                  ALU.subtract).then_inc(s_lo, 1)

            def low(dst, src, high, done):
                dve.tensor_tensor(dst, src, as_f32(high), ALU.subtract).then_inc(done, 1)

            def x_low(q):
                for b in range(4):
                    dve.wait_ge(xt_h, 4 * q + b + 1)
                    k = 8 * q + 2 * b
                    low(xt_lo[:, k:k + 2, :], bank[4 + b][:, :].rearrange("p (k t) -> p k t", k=2),
                        xt_hi[:, k:k + 2, :], xt_l)

            def a_low(i):
                for b in range(4):
                    dve.wait_ge(a_h, 4 * i + b + 1)
                    h, g0 = b // 2, b % 2 * 2
                    low(a_lo[:, i, h, g0:g0 + 2, :], bank[4 + b][:, :].rearrange("p (g t) -> p g t", g=2),
                        a_hi[:, i, h, g0:g0 + 2, :], a_l)

            def a_tokens(i):
                for t in range(TT):
                    dve.wait_ge(s_used, GC * (i + 1))
                    for h in range(2):
                        last = dve.tensor_tensor(
                            a_tok[:, i, h, t, :].rearrange("p (g d) -> p g d", g=NKV),
                            bank[2 * i + t][:, :].rearrange("p (g d) -> p g d", g=NKV),
                            pos_sb[:, i, h:h + 1, :].to_broadcast([P, NKV, HD]), ALU.add)
                        last.then_inc(a_in, 1)

            dve.memset(conv[:, :, :], 0.0).then_inc(cv.sem, 1)
            for t in range(TT):
                dve.memset(tok_b[:, t, :], 0.0).then_inc(zc_tok.sem, 1)
            x_low(0)
            for n in range(AHEAD):
                split(n)
            for i in range(2 * GC + 10):
                n = i + AHEAD
                if i < GC and i % 4 == 2 and i < GC - 2:
                    x_low(i // 4 + 1)
                if i == GC:
                    dve.wait_ge(s_small, small)
                    a_tokens(0)
                if i == GC + 2:
                    dve.wait_ge(taps_ps, 1)
                    dve.tensor_copy(taps[:, :, :].rearrange("p k b -> p (k b)"), bank[6][:, 0:48]
                                    ).then_inc(taps_in, 1)
                if i == GC + 4:
                    a_low(0)
                if i == 2 * GC:
                    a_tokens(1)
                if i == 2 * GC + 2:
                    a_low(1)
                if n < 2 * GC:
                    split(n)
                elif n < 2 * GC + 2:
                    split(n, width=16 * NG)
                elif n < PRO:
                    split(n, width=8 * HD)
            dve.wait_ge(c_ps, 1)
            dve.tensor_copy(kc[:, :, :].rearrange("p g n -> p n g"),
                            bank[6][:, 0:NC * NKV].rearrange("p (n g) -> p n g", g=NKV)).then_inc(c_in, 1)
            dve.wait_ge(c_ps, 2)
            dve.tensor_copy(vc[0:NC, :, :], bank[7][0:NC, :].rearrange("p (g d) -> p g d", g=NKV)
                            ).then_inc(c_in, 1)
            for n in range(PRO, PRO + AHEAD):
                split(n)

            def gate(g):
                dve.wait_ge(s_used, chunk_done(g, -1))
                dve.wait_ge(zc_tok.sem, zc_tok.at(g, 0))
                for t in range(TT):
                    dve.tensor_tensor(tok_b[:, t, :], bank[4 + t][:, :], tok_b[:, t, :], ALU.mult
                                      ).then_inc(g_tok.sem, 1)

            def conv_out(g):
                dve.wait_ge(cv.sem, cv.at(g, 0))
                for b in range(2):
                    dve.wait_ge(g_ps.sem, g_ps.at(g, b + 1))
                    v = conv[:, 2 * b:2 * b + 2, :]
                    dve.tensor_tensor(v, bank[6 + b][:, :].rearrange("p (f t) -> p f t", f=2), v, ALU.mult
                                      ).then_inc(y_in.sem, 1)

            def conv_low(g, block0):
                for b in range(2):
                    dve.wait_ge(y_hi.sem, y_hi.at(g, b + 1))
                    at = bass.ds(block0 + 2 * b, 2)
                    low(mix_lo[:, at, :], conv[:, 2 * b:2 * b + 2, :], mix_hi[:, at, :], y_lo.sem)

            with dve.Fori(0, NKV) as g:
                for i in range(TURN):
                    if i == 0:
                        gate(g)
                    if i == 3:
                        conv_out(g)
                    if i == 4:
                        conv_low(g, g * 4 + 12)
                    if i == GC * (ZA + 1) + 3:
                        dve.wait_ge(z_ps.sem, z_ps.at(g, 2))
                        dve.tensor_copy(z_t[:, 2:4, :], bank[7][:, :].rearrange("p (r t) -> p r t", r=2)
                                        ).then_inc(z_in.sem, 1)
                    if i == GC * (KV + 1) + 3:
                        dve.wait_ge(k_ps.sem, k_ps.at(g, 1))
                        dve.tensor_copy(k_t[:, :, :], bank[6][:, :].rearrange("p (b t) -> p b t", b=2)
                                        ).then_inc(k_in.sem, 1)
                    if i == GC * (Q + 1) + 3:
                        dve.wait_ge(q_ps.sem, q_ps.at(g, 2))
                        dve.tensor_copy(q_t[:, 2:4, :], bank[7][:, :].rearrange("p (r t) -> p r t", r=2)
                                        ).then_inc(q_in.sem, 1)
                    if i == I_CMP:
                        dve.wait_ge(sc_ps.sem, sc_ps.at(g, 1))
                        scores = bank[7][:, 0:GQA * TT * 16].rearrange(
                            "p (r t n) -> p r t n", r=GQA, t=TT)[:, :, :, 0:NC]
                        for r in range(GQA):
                            last = dve.tensor_tensor(sc[:, r], scores[:, r], c_neg[:, :, :], ALU.add)
                        last.then_inc(sc_v.sem, 1)
                        dve.wait_ge(sc_v.sem, sc_v.at(g, 1))
                        flat = sc[:, :, :, :].rearrange("p r t n -> p (r t) n")
                        dve.tensor_reduce(c_max[:, :, :].rearrange("p r t -> p (r t)"), flat, AX.X, ALU.max
                                          ).then_inc(sc_v.sem, 1)
                        dve.wait_ge(sc_v.sem, sc_v.at(g, 2))
                        dve.tensor_tensor(flat, flat, over_keys(c_max), ALU.subtract).then_inc(sc_v.sem, 1)
                    if i == I_CMP + 2:
                        dve.wait_ge(ec_in.sem, ec_in.at(g, 1))
                        flat = ec[:, :, :, :].rearrange("p r t n -> p (r t) n")
                        dve.tensor_reduce(c_sum[:, :, :].rearrange("p r t -> p (r t)"), flat, AX.X, ALU.add
                                          ).then_inc(pc_v.sem, 1)
                        dve.wait_ge(pc_v.sem, pc_v.at(g, 1))
                        dve.reciprocal(c_rcp[:, :, :], c_sum[:, :, :]).then_inc(pc_v.sem, 1)
                        dve.wait_ge(pc_v.sem, pc_v.at(g, 2))
                        dve.wait_ge(group_in.sem, group_in.at(g, 4))
                        dve.tensor_tensor(c_fac[:, :, :], c_rcp[:, :, :],
                                          gates_g[:, :, :].rearrange("p t (r b) -> p r t b", b=3)[:, :, :, 0],
                                          ALU.mult).then_inc(pc_v.sem, 1)
                        dve.wait_ge(pc_v.sem, pc_v.at(g, 3))
                        dve.tensor_tensor(flat, flat, over_keys(c_fac), ALU.mult).then_inc(pc_v.sem, 1)
                        dve.wait_ge(pc_v.sem, pc_v.at(g, 4))
                        for r in range(GQA):
                            last = dve.tensor_tensor(ec[:, r], ec[:, r], c_ok[:, :, :], ALU.mult)
                        last.then_inc(pc_v.sem, 1)
                    for r in range(GQA):
                        if i == I_S + PERIOD * r:
                            for t in range(TT):
                                dve.wait_ge(s_ps.sem, s_ps.at(g, 2 * r + t + 1))
                                dve.tensor_reduce(s_max[:, t, :], bank[4 + t][:, 0:2 * (t + 1) * P].rearrange(
                                    "p (b k) -> p b k", b=2), AX.X, ALU.max).then_inc(mx_v.sem, 1)
                            dve.wait_ge(mx_v.sem, mx_v.at(g, 2 * r + 2))
                            dve.tensor_scalar(s_neg[:, :, :], s_max[:, :, :], -SCALE, None, ALU.mult
                                              ).then_inc(neg_v.sem, 1)
                        if i == I_S + PERIOD * r + 2:
                            dve.wait_ge(exp_in.sem, exp_in.at(g, r + 1))
                            dve.reciprocal(s_rcp[:, :, :], s_sum[:, :, :]).then_inc(rcp_v.sem, 1)
                            dve.wait_ge(rcp_v.sem, rcp_v.at(g, 2 * r + 1))
                            dve.tensor_tensor(s_fac[:, :, :], s_rcp[:, :, :],
                                              gates_g[:, :, 3 * r + 1:3 * r + 3], ALU.mult
                                              ).then_inc(rcp_v.sem, 1)
                            dve.wait_ge(rcp_v.sem, rcp_v.at(g, 2 * r + 2))
                            for t in range(TT):
                                for b in range(2):
                                    v = prob[:, t, b, 0:(t + 1) * P]
                                    last = dve.tensor_scalar(v, v, s_fac[:, t, b:b + 1], None, ALU.mult)
                                last.then_inc(p_in.sem, 1)
                        if i == I_T + PERIOD * r:
                            dve.wait_ge(p_ps.sem, p_ps.at(g, 2 * r + 2))
                            v = bank[7][:, :].rearrange("p (b k q) -> p b k q", b=2, k=2)
                            dve.tensor_copy(p_t0[:, :, P:T], v[:, :, 0, :]).then_inc(pt_v.sem, 1)
                            dve.tensor_copy(p_t1[:, :, :], v[:, :, 1, :]).then_inc(pt_v.sem, 1)
                        if i == I_V + PERIOD * r:
                            dve.wait_ge(o_ps.sem, o_ps.at(g, r + 1))
                            dve.tensor_tensor(att[:, :], bank[6][:, 0:T], z_t[:, r, :], ALU.mult
                                              ).then_inc(o_in.sem, 1)
                        if i == I_V + PERIOD * r + 1:
                            dve.wait_ge(o_hi.sem, o_hi.at(g, r + 1))
                            at = bass.ds(g * 4 + r, 1)
                            low(mix_lo[:, at, :].rearrange("p a t -> p (a t)"), att[:, :],
                                mix_hi[:, at, :].rearrange("p a t -> p (a t)"), o_lo.sem)
                    if i == GC * (CG + 1):
                        dve.wait_ge(s_used, chunk_done(g, CG))
                        dve.wait_ge(h_tok.sem, h_tok.at(g, 2))
                        for t in range(TT):
                            dve.tensor_tensor(tok_a[:, t, :], bank[2 * PAIR[CG] + t][:, :], tok_a[:, t, :],
                                              ALU.mult).then_inc(u_tok.sem, 1)
                    if i == I_U:
                        dve.wait_ge(group_in.sem, group_in.at(g, 4))
                        for tap in range(3):
                            for f in range(4):
                                u = bank[6 + f // 2][:, f % 2 * T:(f % 2 + 1) * T]
                                w = taps_g[:, 2 - tap, f:f + 1]
                                c = conv[:, f, tap:T]
                                if tap == 0:
                                    dve.wait_ge(u_ps.sem, u_ps.at(g, f // 2 + 1))
                                    dve.tensor_scalar(c, u, w, None, ALU.mult).then_inc(cv.sem, 1)
                                else:
                                    dve.wait_ge(cv.sem, cv.at(g, 4 * tap + f - 3))
                                    dve.scalar_tensor_tensor(out=c, in0=u[:, 0:T - tap], scalar=w, in1=c,
                                                             op0=ALU.mult, op1=ALU.add).then_inc(cv.sem, 1)
                    split(PRO + i + AHEAD, g)

            gate(NKV)
            conv_out(NKV)
            conv_low(NKV, KT - 4)
            dve.wait_ge(y_lo.sem, y_lo.at(NKV, 2))
            dve.memset(eps[:, :], EPS).then_inc(y_sum, 4)

            def chunk_sums(c, b, loads, done, before):
                dve.wait_ge(s_used, done)
                dve.wait_ge(res_in[b], loads)
                for t in range(TT):
                    dve.scalar_tensor_tensor(out=y[:, t, bass.ds(c * W, W)], in0=x_res[b][:, t, :],
                                             scalar=ALPHA, in1=bank[2 * (1 - b) + t][:, :],
                                             op0=ALU.mult, op1=ALU.add).then_inc(y_sum, 1)
                for t in range(TT):
                    dve.wait_ge(y_sum, before + (t + 1))
                    st = stats[:, t, bass.ds(c, 1), :].rearrange("p a s -> p (a s)")
                    dve.bn_stats(st, y[:, t, bass.ds(c * W, W)]).then_inc(y_stat, 1)

            for i in range(GC):
                split(OUT0 + i + AHEAD)
            with dve.Fori(0, NOUT // 2 - 1) as c2:
                for b in range(2):
                    chunk_sums(c2 * 2 + b, b, c2 * 16 + 16, c2 * (2 * GC) + (OUT0 + (b + 1) * GC),
                               c2 * 4 + (4 + 2 * b))
                    for i in range(GC):
                        split(OUT0 + (b + 1) * GC + i + AHEAD, c2, 2 * GC)
            for b in range(2):
                c = NOUT - 2 + b
                chunk_sums(c, b, c // 2 * 16 + 16, OUT0 + (c + 1) * GC, 4 + 2 * c)
                if b == 0:
                    for i in range(GC - AHEAD):
                        split(OUT0 + (NOUT - 1) * GC + i + AHEAD)

            dve.wait_ge(y_stat, 2 * NOUT)
            for t in range(TT):
                dve.bn_aggr(mv[:, t, :], stats[:, t, :, :].rearrange("p c s -> p (c s)")
                            ).then_inc(mv_in, 1)
            dve.wait_ge(std_in, 1)
            dve.reciprocal(rstd[:, :], std[:, :]).then_inc(rstd_in, 1)
            dve.wait_ge(rstd_in, 1)
            dve.scalar_tensor_tensor(out=shift[:, :], in0=mv[:, :, 0], scalar=-1.0, in1=rstd[:, :],
                                     op0=ALU.mult, op1=ALU.mult).then_inc(shift_in, 1)
            dve.wait_ge(norm_in, 32)
            for i in range(FIN):
                t, c0 = divmod(i * FW, D)
                v = y[:, t, c0:c0 + FW]
                dve.wait_ge(n_scaled, i + 1)
                dve.tensor_tensor(v, v, gamma[:, c0:c0 + FW], ALU.mult).then_inc(n_gamma, 1)
                if i in FIN_DVE:
                    dve.wait_ge(n_gamma, i + 1)
                    dve.tensor_tensor(v, v, beta[:, c0:c0 + FW], ALU.add).then_inc(n_out_v, 1)

        @block.tensor
        def _(pe):
            def granule(s, hi, lo, k0, pair, width, tiles, first, last):
                for k in range(tiles):
                    wh = w_hi[s][:, k * width:(k + 1) * width]
                    wl = w_lo[s][:, k * width:(k + 1) * width]
                    for t in range(TT):
                        xh, xl = (m[:, k0 + k, t * P:(t + 1) * P] for m in (hi, lo))
                        acc = bank[2 * pair + t][:, 0:width]
                        pe.matmul(acc, xh, wl, start=first and k == 0, stop=False)
                        pe.matmul(acc, xh, wh, start=False, stop=False)
                        mm = pe.matmul(acc, xl, wh, start=False, stop=last and k == tiles - 1)
                mm.then_inc(s_used, 1)

            def transpose(dst, src):
                rows = src.shape[0]
                return pe.transpose(dst, src, ident[0:rows, 0:rows])

            def x_transposes(q):
                pe.wait_ge(x_in[q], 16)
                for b in range(4):
                    if q:
                        pe.wait_ge(xt_l, 4 * (q - 1) + b + 1)
                    for k in range(2):
                        kt = 8 * q + 2 * b + k
                        for t in range(TT):
                            last = transpose(bank[4 + b][:, k * T + t * P:k * T + (t + 1) * P],
                                             x_tok[:, t, kt * P:(kt + 1) * P])
                    last.then_inc(xt_ps, 1)

            def a_transposes(i):
                pe.wait_ge(a_in, 4 * i + 4)
                for b in range(4):
                    if i == 0:
                        pe.wait_ge(xt_l, 12 + b + 1)
                    else:
                        pe.wait_ge(a_l, b + 1)
                    h = b // 2
                    for gg in range(2):
                        g = b % 2 * 2 + gg
                        for t in range(TT):
                            last = transpose(bank[4 + b][:, gg * T + t * P:gg * T + (t + 1) * P],
                                             a_tok[:, i, h, t, g * HD:(g + 1) * HD])
                    last.then_inc(a_ps, 1)

            def chunk_granules(base, g, per, hi, lo, pair, steps):
                for j in range(GC):
                    steps(j)
                    n = base + j
                    pe.wait_ge(s_lo, g * per + (n + 1))
                    granule(n % RING, hi, lo, GK * j, pair, W, GK, j == 0, j == GC - 1)

            pe.wait_ge(s_const, 5)
            x_transposes(0)

            def chunk0_steps(j):
                if j % 4 == 2 and j < GC - 2:
                    x_transposes(j // 4 + 1)
                pe.wait_ge(xt_l, j + 1)

            def chunk1_steps(j):
                if j == 2:
                    pe.wait_ge(s_small, small)
                    pe.wait_ge(xt_l, 16)
                    transpose(bank[6][:, 0:48], conv_rows[:, :]).then_inc(taps_ps, 1)
                if j == 4:
                    pe.wait_ge(taps_in, 1)
                    a_transposes(0)

            chunk_granules(0, 0, 0, xt_hi, xt_lo, 0, chunk0_steps)
            chunk_granules(GC, 0, 0, xt_hi, xt_lo, 1, chunk1_steps)
            pe.wait_ge(a_in, 4)
            for j in range(2):
                n = 2 * GC + j
                pe.wait_ge(s_lo, n + 1)
                granule(n % RING, xt_hi, xt_lo, 16 * j, 0, NG, 16, j == 0, j == 1)
            a_transposes(1)
            pe.wait_ge(a_in, 8)
            for i in range(2):
                for j in range(4):
                    n = 2 * GC + 2 + 4 * i + j
                    pe.wait_ge(s_lo, n + 1)
                    pe.wait_ge(a_l, 4 * i + 4)
                    for k in range(8):
                        pos_in = 8 * j + k
                        h = pos_in // DC
                        tokens = slice(pos_in, pos_in + DC * (NC - 1) + 1, DC)
                        ah, al = (m[:, i, h, :, tokens].rearrange("p g n -> p n g") for m in (a_hi, a_lo))
                        wh, wl = (m[n % RING][:, k * HD:(k + 1) * HD] for m in (w_hi, w_lo))
                        acc = bank[2 + i][:, 0:NC * NKV].rearrange("p (n g) -> p n g", g=NKV)
                        pe.matmul(acc, wh, al, start=pos_in == 0, stop=False)
                        pe.matmul(acc, wh, ah, start=False, stop=False)
                        mm = pe.matmul(acc, wl, ah, start=False, stop=pos_in == LC - 1)
                    mm.then_inc(s_used, 1)
            pe.wait_ge(hid_in, 1)
            pe.wait_ge(a_l, 8)
            pe.matmul(bank[6][:, 0:NC * NKV], w2_sb[:, 0, :], hid[:, 0].rearrange("p n g -> p (n g)"),
                      start=True, stop=True).then_inc(c_ps, 1)
            pe.wait_ge(hid_in, 2)
            for g in range(NKV):
                mm = pe.matmul(bank[7][0:NC, g * HD:(g + 1) * HD], hid[:, 1, :, g], w2_sb[:, 1, :],
                               start=True, stop=True)
            mm.then_inc(c_ps, 1)

            def gate_transposes(g):
                pe.wait_ge(cv.sem, cv.at(g, 0))
                pe.wait_ge(g_tok.sem, g_tok.at(g, 2))
                for b in range(2):
                    for f in range(2):
                        for t in range(TT):
                            last = transpose(bank[6 + b][:, f * T + t * P:f * T + (t + 1) * P],
                                             tok_b[:, t, (2 * b + f) * P:(2 * b + f + 1) * P])
                    last.then_inc(g_ps.sem, 1)

            def heads_transposes(done):
                for b in range(2):
                    for f in range(2):
                        for t in range(TT):
                            last = transpose(bank[6 + b][:, f * T + t * P:f * T + (t + 1) * P],
                                             tok_a[:, t, (2 * b + f) * P:(2 * b + f + 1) * P])
                    last.then_inc(done.sem, 1)

            def group_steps(g, i):
                if i == 3:
                    gate_transposes(g)
                if i == GC * (ZA + 1) + 3:
                    pe.wait_ge(za_tok.sem, za_tok.at(g, 2))
                    pe.wait_ge(y_in.sem, y_in.at(g, 2))
                    heads_transposes(z_ps)
                if i == GC * (KV + 1) + 3:
                    pe.wait_ge(kv_tok.sem, kv_tok.at(g, 2))
                    pe.wait_ge(z_in.sem, z_in.at(g, 2))
                    for b in range(2):
                        for t in range(TT):
                            last = transpose(bank[6][:, b * T + t * P:b * T + (t + 1) * P],
                                             tok_b[:, t, 2 * b * P:(2 * b + 1) * P])
                    last.then_inc(k_ps.sem, 1)
                if i == GC * (Q + 1) + 3:
                    pe.wait_ge(q_tok.sem, q_tok.at(g, 2))
                    pe.wait_ge(k_in.sem, k_in.at(g, 1))
                    heads_transposes(q_ps)
                if i == I_CMP:
                    pe.wait_ge(q_in.sem, q_in.at(g, 2))
                    pe.wait_ge(group_in.sem, group_in.at(g, 4))
                    for r in range(GQA):
                        for t in range(TT):
                            c0 = (r * TT + t) * 16
                            mm = pe.matmul(bank[7][:, c0:c0 + NC], q_t[:, r, t * P:(t + 1) * P], kc_g[:, :],
                                           start=True, stop=True)
                    mm.then_inc(sc_ps.sem, 1)
                for r in range(GQA):
                    if i == I_S + PERIOD * r:
                        if r:
                            pe.wait_ge(exp_in.sem, exp_in.at(g, r))
                        else:
                            pe.wait_ge(g_tok.sem, g_tok.at(g, 2))
                        for t in range(TT):
                            keys = (t + 1) * P
                            for b in range(2):
                                acc = bank[4 + t][:, b * keys:(b + 1) * keys]
                                pe.matmul(acc, q_t[:, r, t * P:(t + 1) * P], k_t[:, b, 0:keys],
                                          start=True, stop=False)
                                mm = pe.matmul(acc[:, t * P:keys], ident_b[:, :], causal[:, :],
                                               start=False, stop=True)
                            mm.then_inc(s_ps.sem, 1)
                    if i == I_T + PERIOD * r:
                        pe.wait_ge(p_in.sem, p_in.at(g, 2 * r + 2))
                        if r == 0:
                            pe.wait_ge(pc_v.sem, pc_v.at(g, 5))
                        else:
                            pe.wait_ge(o_in.sem, o_in.at(g, r))
                        for b in range(2):
                            transpose(bank[6][:, b * P:(b + 1) * P], prob[:, 0, b, 0:P])
                        for t in range(TT):
                            last = transpose(bank[6][0:NC, (2 + t) * P:(3 + t) * P], ec[:, r, t, :])
                        last.then_inc(p_ps.sem, 1)
                        for b in range(2):
                            for k in range(TT):
                                c0 = (2 * b + k) * P
                                last = transpose(bank[7][:, c0:c0 + P], prob[:, 1, b, k * P:(k + 1) * P])
                        last.then_inc(p_ps.sem, 1)
                    if i == I_V + PERIOD * r:
                        pe.wait_ge(pt_a.sem, pt_a.at(g, 2 * r + 2))
                        pe.wait_ge(pt_v.sem, pt_v.at(g, 2 * r + 2))
                        acc = bank[6][:, 0:T]
                        pe.matmul(acc, vc_g[0:NC, :], pc_t[0:NC, :], start=True, stop=False)
                        for b in range(2):
                            v = tok_b[:, :, (2 * b + 1) * P:(2 * b + 2) * P]
                            pe.matmul(acc, v[:, 0, :], p_t0[:, b, :], start=False, stop=False)
                            mm = pe.matmul(acc[:, P:T], v[:, 1, :], p_t1[:, b, :], start=False, stop=b == 1)
                        mm.then_inc(o_ps.sem, 1)
                if i == GC * ZC:
                    pe.wait_ge(h_tok.sem, h_tok.at(g, 2))
                if i == I_U:
                    pe.wait_ge(u_tok.sem, u_tok.at(g, 2))
                    pe.wait_ge(o_in.sem, o_in.at(g, GQA))
                    heads_transposes(u_ps)

            pe.wait_ge(c_in, 2)
            pe.wait_ge(gates_in, 2)
            with pe.Fori(0, NKV) as g:
                for c in range(CH):
                    chunk_granules(PRO + c * GC, g, TURN, xt_hi, xt_lo, PAIR[c],
                                   lambda j, c=c: group_steps(g, c * GC + j))

            gate_transposes(NKV)

            def out_steps(j):
                if j == 14:
                    pe.wait_ge(y_lo.sem, y_lo.at(NKV, 2))

            with pe.Fori(0, NOUT // 2) as c2:
                for b in range(2):
                    pe.wait_ge(y_sum, c2 * 4 + (2 * b + 2))
                    chunk_granules(OUT0 + b * GC, c2, 2 * GC, mix_hi, mix_lo, 1 - b, out_steps)


NAMES = ["x", "w_in", "conv_w", "cmp_pos_k", "cmp_w1_k", "cmp_w2_k", "cmp_pos_v", "cmp_w1_v",
         "cmp_w2_v", "w_out", "ln_g", "ln_b"]


def kernel(**inputs):
    import concourse.bacc as bacc
    from concourse.bass_utils import run_bass_kernel_spmd as run

    nc = bacc.Bacc("TRN2", target_bir_lowering=False, num_devices=1, dynamic_dma_scratch_size=8192)
    arrays, args = {}, []
    for name in NAMES:
        a = np.ascontiguousarray(inputs[name])
        arrays[f"in_{name}"] = a
        args.append(nc.dram_tensor(f"in_{name}", a.shape, mybir.dt.from_np(a.dtype),
                                   kind="ExternalInput").ap())
    o = nc.dram_tensor("out_y", (1, T, D), F32, kind="ExternalOutput").ap()
    build(nc, *args, o)
    return run(nc, [arrays], core_ids=[0]).results[0]["out_y"]
```

```python
from contextlib import ExitStack

import numpy as np

import concourse.bass as bass
from concourse import mybir

F32 = mybir.dt.float32
F32R = mybir.dt.float32r
BF16 = mybir.dt.bfloat16
ALU = mybir.AluOpType
ACT = mybir.ActivationFunctionType
AX = mybir.AxisListType

P = 128
D = 4096
T = 256
TT = T // P
KT = D // P
W = 512
WC = 2048
HD = 128
NKV = 4
GQA = 4
WKV = NKV * HD
LC, DC = 32, 16
NC = T // DC - LC // DC + 1
SCALE = float(HD) ** -0.5
ALPHA = 2.0 ** 0.25
EPS = 1e-5
NEG = -1e30

C_H, C_BG, C_CG, C_ZC, C_Q = (WC * i for i in range(5))
C_KCMP = 5 * WC
C_VCMP = C_KCMP + WKV
C_KV = C_VCMP + WKV
C_ZA = C_KV + 4 * WKV
C_GATE = C_ZA + WC
NG = 48

GK = 2
GC = KT // GK
RING = 4
AHEAD = RING - 1
MLP_K = GC + 10
GATE0 = 2 * GC + 4
MLP_V = GATE0 + 3
PRO = GATE0 + 8
XP = 8
CH = 7
TURN = CH * GC
OUT0 = PRO + NKV * TURN
NOUT = D // W
LAST = OUT0 + NOUT * GC
assert TURN % RING == 0 and GC % RING == 0

ZA, KV, Q, H, CG, ZC, BG = range(CH)
PAIR = (1, 0, 1, 0, 1, 0, 2)
I_CMP, I_S, I_T, I_V, PERIOD = 54, 56, 60, 63, 10
I_U = CH * GC - 14
COLS = {ZA: C_ZA, Q: C_Q, H: C_H, CG: C_CG, ZC: C_ZC, BG: C_BG}


FW = 1024
FIN = T // P * D // FW
FIN_T = FIN // TT
FIN_POOL = (0, 1, 2, 5)
FIN_DVE = tuple(i for i in range(FIN) if i not in FIN_POOL)


class Signal:

    def __init__(self, sem, per=0, before=0):
        self.sem, self.per, self.before = sem, per, before

    def at(self, g, k):
        return g * self.per + (self.before + k)


def chunk_done(g, c):
    return g * TURN + (PRO + GC * (c + 1))


def landed_at(n, g=0, per=TURN):
    first, twice = PRO + KV * GC, GC // RING
    if n >= OUT0:
        extra, again = NKV * twice, 0
    else:
        extra, again = min(max((n - first) // RING + 1, 0), twice), twice
    return g * (16 * (per // RING + again)) + 16 * (n // RING + 1 + extra)


def over_keys(m):
    return m[:, :, :].rearrange("p r (t a) -> p (r t) a", a=1).to_broadcast([P, GQA * TT, NC])


def build(nc, x, w_in, conv_w, pos_k, w1_k, w2_k, pos_v, w1_v, w2_v, w_out, ln_g, ln_b, out):
    x, out = x[0], out[0]
    w_in, conv_w, w_out = w_in[0], conv_w[0], w_out[0]
    pos, w1, w2 = (pos_k[0], pos_v[0]), (w1_k[0], w1_v[0]), (w2_k[0], w2_v[0])

    with ExitStack() as ctx:
        top = [(nc.sbuf_base + 31) // 32 * 32]

        def region(kib):
            at = top[0]
            top[0] += int(kib * 1024)
            return at

        def place(name, shape, dt, at):
            return nc.alloc_sbuf_tensor_at(name, shape, dt, offset=at)

        def own(name, shape, dt):
            size = int(np.prod(shape[1:])) * (2 if dt == BF16 else 4)
            return place(name, shape, dt, region((size + 31) // 32 * 32 / 1024))

        r_x = region(64)
        xt_hi = place("xt_hi", [P, KT, T], F32R, r_x)
        xt_lo = place("xt_lo", [P, KT, T], F32R, r_x + 32 * 1024)
        y = place("y", [P, TT, D], F32, r_x)
        gamma = place("gamma", [P, D], F32, r_x + 32 * 1024)
        beta = place("beta", [P, D], F32, r_x + 48 * 1024)

        r_m = region(64)
        mix_hi = place("mix_hi", [P, KT, T], F32R, r_m)
        mix_lo = place("mix_lo", [P, KT, T], F32R, r_m + 32 * 1024)
        x_tok = place("x_tok", [P, TT, D], F32, r_m)
        a_tok = place("a_tok", [P, 2, 2, TT, W], F32, r_m)
        a_t = place("a_t", [P, 2, 2, 2, NKV, T], F32R, r_m + 32 * 1024)

        raw = [own(f"raw{i}", [P, GK * W], F32) for i in range(RING)]
        parts = [own(f"parts{i}", [P, 2, GK * W], F32R) for i in range(RING)]
        w_hi, w_lo = ([w[:, i, :] for w in parts] for i in range(2))

        r_s = top[0]
        tok_a = own("tok_a", [P, TT, W], F32)
        tok_b = own("tok_b", [P, TT, W], F32)
        k_t = own("k_t", [P, 2, T], F32)
        q_t = own("q_t", [P, GQA, T], F32)
        z_t = own("z_t", [P, GQA, T], F32)
        r_prob = top[0]
        prob = own("prob", [P, TT, 2, T], F32)
        p_t0 = own("p_t0", [P, 2, T], F32)
        p_t1 = own("p_t1", [P, 2, P], F32)
        pc_t = own("pc_t", [P, T], F32)
        conv = place("conv", [P, 4, T], F32, r_prob)
        att = own("att", [P, T], F32)
        ident = own("ident", [P, P], F32)
        ident_b = own("ident_b", [P, P], BF16)
        causal = own("causal", [P, P], BF16)
        c_neg = own("c_neg", [P, TT, NC], F32)
        c_ok = own("c_ok", [P, TT, NC], F32)
        taps = own("taps", [P, 3, 16], F32)
        taps_g = own("taps_g", [P, 3, 4], F32)
        gates = own("gates", [P, TT, NG], F32)
        gates_g = own("gates_g", [P, TT, GQA * 3], F32)
        kc = own("kc", [P, NKV, DC], F32)
        kc_g = own("kc_g", [P, DC], F32)
        vc = own("vc", [P, NKV, HD], F32)
        vc_g = own("vc_g", [P, HD], F32)
        sc = own("sc", [P, GQA, TT, NC], F32)
        ec = own("ec", [P, GQA, TT, NC], F32)
        c_max = own("c_max", [P, GQA, TT], F32)
        c_sum = own("c_sum", [P, GQA, TT], F32)
        c_rcp = own("c_rcp", [P, GQA, TT], F32)
        c_fac = own("c_fac", [P, GQA, TT], F32)
        s_max = own("s_max", [P, TT, 2], F32)
        s_neg = own("s_neg", [P, TT, 2], F32)
        s_sum = own("s_sum", [P, TT, 2], F32)
        s_rcp = own("s_rcp", [P, TT, 2], F32)
        s_fac = own("s_fac", [P, TT, 2], F32)
        assert top[0] <= nc.sbuf_usable_end, (top[0], nc.sbuf_usable_end)

        conv_rows = place("conv_rows", [48, P], F32, r_s + 8 * 1024)
        pos_sb = place("pos_sb", [P, 2, 2, HD], F32, r_s + 9 * 1024)
        w2_sb = place("w2_sb", [P, 2, HD], F32, r_s + 11 * 1024)
        hid = place("hid", [P, 2, NKV, DC], F32, r_s + 12 * 1024)
        hid_4 = place("hid_4", [P, 2, 2, HD], F32, r_s)
        gate_t = place("gate_t", [P, T], F32, r_s + 2048)
        fold = place("fold", [P, P // 2], F32, r_s + 3072)
        x_res = [place(f"x_res{i}", [P, TT, W], F32, r_s + 4096 * i) for i in range(2)]
        stats = place("stats", [P, TT, NOUT, 6], F32, r_s + 8192)
        mv = place("mv", [P, TT, 2], F32, r_s + 9 * 1024)
        eps = place("eps", [P, 1], F32, r_s + 9 * 1024 + 64)
        std = place("std", [P, TT], F32, r_s + 9 * 1024 + 128)
        rstd = place("rstd", [P, TT], F32, r_s + 9 * 1024 + 192)
        shift = place("shift", [P, TT], F32, r_s + 9 * 1024 + 256)

        bank = [ctx.enter_context(nc.psum_tensor(f"bank{i}", [P, W], F32)) for i in range(8)]

        def sem(name):
            return ctx.enter_context(nc.semaphore(name))

        landed = [sem(f"landed{i}") for i in range(RING)]
        s_hi = sem("s_hi")
        s_lo = sem("s_lo")
        s_used = sem("s_used")
        s_const = sem("s_const")
        s_pool = sem("s_pool")
        s_small = sem("s_small")
        x_in = [sem(f"x_in{i}") for i in range(XP)]
        xt_ps, xt_h, xt_l = sem("xt_ps"), sem("xt_h"), sem("xt_l")
        taps_ps, taps_in = sem("taps_ps"), sem("taps_in")
        a_in = sem("a_in")
        a_ps, a_h, a_l = sem("a_ps"), sem("a_h"), sem("a_l")
        a_pad = sem("a_pad")
        hid_4_in, hid_ps, hid_in = sem("hid_4_in"), sem("hid_ps"), sem("hid_in")
        gate_t_in, gates_ps, gates_in = sem("gate_t_in"), sem("gates_ps"), sem("gates_in")
        kc_ps, kc_in, vc_ps, vc_in = sem("kc_ps"), sem("kc_in"), sem("vc_ps"), sem("vc_in")

        group_in = Signal(sem("group_in"), 4)
        g_tok = Signal(sem("g_tok"), 2)
        g_ps = Signal(sem("g_ps"), 2)
        y_in = Signal(sem("y_in"), 2)
        y_hi = Signal(sem("y_hi"), 2)
        y_lo = Signal(sem("y_lo"), 2)
        za_tok = Signal(sem("za_tok"), 2)
        z_ps = Signal(sem("z_ps"), 2)
        z_in = Signal(sem("z_in"), 2)
        kv_tok = Signal(sem("kv_tok"), 2)
        k_ps = Signal(sem("k_ps"), 1)
        k_in = Signal(sem("k_in"), 1)
        q_tok = Signal(sem("q_tok"), 2)
        q_ps = Signal(sem("q_ps"), 2)
        q_in = Signal(sem("q_in"), 2)
        sc_ps = Signal(sem("sc_ps"), 1)
        sc_v = Signal(sem("sc_v"), 3)
        ec_in = Signal(sem("ec_in"), 1)
        pc_v = Signal(sem("pc_v"), 5)
        s_ps = Signal(sem("s_ps"), 2 * GQA)
        mx_v = Signal(sem("mx_v"), 2 * GQA)
        neg_v = Signal(sem("neg_v"), GQA)
        exp_in = Signal(sem("exp_in"), GQA)
        rcp_v = Signal(sem("rcp_v"), 2 * GQA)
        p_in = Signal(sem("p_in"), 2 * GQA)
        p_ps = Signal(sem("p_ps"), 2 * GQA)
        pt_a = Signal(sem("pt_a"), 2 * GQA)
        pt_v = Signal(sem("pt_v"), 2 * GQA)
        o_ps = Signal(sem("o_ps"), GQA)
        o_in = Signal(sem("o_in"), GQA)
        o_hi = Signal(sem("o_hi"), GQA)
        o_lo = Signal(sem("o_lo"), GQA)
        h_tok = Signal(sem("h_tok"), 2)
        u_tok = Signal(sem("u_tok"), 2)
        zc_tok = Signal(sem("zc_tok"), 2, 2)
        u_ps = Signal(sem("u_ps"), 2)
        cv = Signal(sem("cv"), 12, 1)

        res_in = [sem(f"res_in{i}") for i in range(2)]
        norm_in = sem("norm_in")
        y_sum = sem("y_sum")
        y_stat = sem("y_stat")
        out_tile0 = sem("out_tile0")
        mv_in, std_in = sem("mv_in"), sem("std_in")
        rstd_in, shift_in = sem("rstd_in"), sem("shift_in")
        n_scaled, n_gamma = sem("n_scaled"), sem("n_gamma")
        n_out_v, n_out_p = sem("n_out_v"), sem("n_out_p")
        stored = sem("stored")
        small = 16 * (1 + 2 * (P // DC + 1))

        block = ctx.enter_context(nc.Block())

        def as_f32(ap):
            return ap.bitcast(F32)

        def a_block(i, part, b):
            h, g0 = b // 2, b % 2 * 2
            src = bank[4 + b][:, :].rearrange("p (g t) -> p g t", g=2)
            return a_t[:, i, h, part, g0:g0 + 2, 0:T - h * DC], src[:, :, h * DC:T]

        @block.sync
        def _(sp):
            def load(slot, src, shape):
                k, c = shape
                dst = raw[slot][:, 0:k * c].rearrange("p (k c) -> p k c", k=k)
                sp.dma_start(dst, src).then_inc(landed[slot], 16)

            def rows(w, r0, n, c0, width):
                return w[bass.ds(r0, n * P), bass.ds(c0, width)].rearrange("(k p) c -> p k c", p=P)

            def first_loads(n):
                if n < GC:
                    load(n % RING, rows(w_in, n * GK * P, GK, C_KCMP, W), (GK, W))
                elif MLP_K <= n < MLP_K + 4:
                    load(n % RING, rows(w1[0], (n - MLP_K) * 8 * HD, 8, 0, HD), (8, HD))
                elif n < GATE0:
                    j = n - GC - (4 if n >= MLP_K else 0)
                    load(n % RING, rows(w_in, j * GK * P, GK, C_VCMP, W), (GK, W))
                elif MLP_V <= n < MLP_V + 4:
                    load(n % RING, rows(w1[1], (n - MLP_V) * 8 * HD, 8, 0, HD), (8, HD))
                else:
                    j = n - GATE0 - (4 if n >= MLP_V else 0)
                    load(n % RING, rows(w_in, j * 8 * P, 8, C_GATE + NG - P, P), (8, P))

            for q in range(XP):
                cols = slice(q * D // XP, (q + 1) * D // XP)
                sp.dma_start(x_tok[:, :, cols], x[:, cols].rearrange("(t p) c -> p t c", p=P)
                             ).then_inc(x_in[q], 16)
                if q < RING:
                    first_loads(q)
            for n in range(RING, PRO):
                sp.wait_ge(s_lo, n - AHEAD)
                first_loads(n)

            with sp.Fori(0, NKV) as g:
                for c in range(CH):
                    with sp.Fori(0, GC // RING) as j:
                        for k in range(RING):
                            n = PRO + c * GC + k
                            sp.wait_ge(s_lo, g * TURN + j * RING + (n - AHEAD))
                            r0 = j * (RING * GK * P) + k * GK * P
                            if c == KV:
                                strips = w_in[:, C_KV:C_KV + 4 * WKV].rearrange("r (s c) -> r s c", s=4)
                                for kk in range(GK):
                                    sp.dma_start(
                                        raw[n % RING][:, kk * W:(kk + 1) * W].rearrange(
                                            "p (s c) -> p s c", s=4),
                                        strips[bass.ds(r0 + kk * P, P), :, bass.ds(g * HD, HD)]
                                    ).then_inc(landed[n % RING], 16)
                            else:
                                load(n % RING, rows(w_in, r0, GK, g * W + COLS[c], W), (GK, W))

            with sp.Fori(0, NOUT) as c:
                for half in range(2):
                    with sp.Fori(0, GC // RING // 2) as j:
                        for k in range(RING):
                            n = OUT0 + half * GC // 2 + k
                            sp.wait_ge(s_lo, c * GC + j * RING + (n - AHEAD))
                            r0 = j * (RING * GK * P) + ((1 - half) * WC + k * GK * P)
                            load(n % RING, rows(w_out, r0, GK, c * W, W), (GK, W))

            for i in range(FIN):
                t, c0 = divmod(i * FW, D)
                if i in FIN_POOL:
                    sp.wait_ge(n_out_p, FIN_POOL.index(i) + 1)
                else:
                    sp.wait_ge(n_out_v, FIN_DVE.index(i) + 1)
                sp.dma_start(out[t * P:(t + 1) * P, c0:c0 + FW], y[:, t, c0:c0 + FW]).then_inc(stored, 16)
            sp.wait_ge(stored, 16 * FIN)

        @block.gpsimd
        def _(pool):
            pool.memset(ident[:, :], 0.0).then_inc(s_pool, 1)
            pool.memset(causal[:, :], 0.0).then_inc(s_pool, 1)
            pool.memset(c_neg[:, :, :], 0.0).then_inc(s_pool, 1)
            pool.memset(c_ok[:, :, :], 1.0).then_inc(s_pool, 1)
            pool.memset(fold[:, :], 0.0).then_inc(s_pool, 1)
            pool.wait_ge(s_pool, 5)
            pool.affine_select(out=ident[:, :], in_=ident[:, :], compare_op=ALU.not_equal, fill=1.0,
                               base=0, pattern=[[-1, P]], channel_multiplier=1).then_inc(s_const, 1)
            pool.affine_select(out=causal[:, :], in_=causal[:, :], compare_op=ALU.is_ge, fill=NEG,
                               base=0, pattern=[[-1, P]], channel_multiplier=1).then_inc(s_const, 1)
            for m, fill in ((c_neg, NEG), (c_ok, 0.0)):
                pool.affine_select(out=m[:, :, :], in_=m[:, :, :], compare_op=ALU.is_ge, fill=fill,
                                   base=-(LC - 1), pattern=[[P, TT], [-DC, NC]],
                                   channel_multiplier=1).then_inc(s_const, 1)
            pool.wait_ge(s_const, 4)
            pool.tensor_copy(ident_b[:, :], ident[:, :]).then_inc(s_const, 1)
            for i in range(2):
                for a in range(P // DC):
                    pool.dma_start(pos_sb[a * DC:(a + 1) * DC, i],
                                   pos[i].rearrange("(h b) d -> b h d", h=2)).then_inc(s_small, 16)
                pool.dma_start(w2_sb[:, i], w2[i]).then_inc(s_small, 16)
            pool.dma_start(conv_rows[:, :], conv_w.rearrange("k (b c) -> (k b) c", c=P)
                           ).then_inc(s_small, 16)
            for i in range(2):
                for part in range(2):
                    pool.memset(as_f32(a_t[:, i, 1, part, :, T - DC:T]), 0.0).then_inc(a_pad, 1)
            for half in range(2):
                pool.wait_ge(s_const, 5 + half)
                pool.affine_select(out=fold[:, :], in_=fold[:, :], compare_op=ALU.not_equal, fill=1.0,
                                   base=-half * (P // 2), pattern=[[-1, P // 2]], channel_multiplier=1
                                   ).then_inc(s_const, 1)

            pool.wait_ge(kc_in, 1)
            pool.wait_ge(vc_in, 1)
            pool.wait_ge(gates_in, 1)
            pool.wait_ge(taps_in, 1)
            with pool.Fori(0, NKV) as g:
                pool.wait_ge(cv.sem, cv.at(g, 0))
                for dst, src in ((kc_g[:, :], kc[:, bass.ds(g, 1), :]),
                                 (vc_g[0:NC, :], vc[0:NC, bass.ds(g, 1), :])):
                    pool.tensor_copy(dst, src.rearrange("p a n -> p (a n)")).then_inc(group_in.sem, 1)
                pool.tensor_copy(taps_g[:, :, :], taps[:, :, bass.ds(g * 4, 4)]).then_inc(group_in.sem, 1)
                pool.tensor_copy(gates_g[:, :, :], gates[:, :, bass.ds(g * (3 * GQA), 3 * GQA)]
                                 ).then_inc(group_in.sem, 1)

            pool.wait_ge(s_used, OUT0)
            for dst, src in ((gamma, ln_g), (beta, ln_b)):
                pool.dma_start(dst[:, :], src.to_broadcast([P, D])).then_inc(norm_in, 16)
            with pool.Fori(0, NOUT // 2) as c2:
                for b in range(2):
                    pool.wait_ge(y_sum, c2 * 4 + (2 * b + 2))
                    pool.dma_start(x_res[b][:, :, :],
                                   x[:, bass.ds(c2 * (2 * W) + b * W, W)].rearrange(
                                       "(t p) c -> p t c", p=P)).then_inc(res_in[b], 16)

            for i in FIN_POOL:
                t, c0 = divmod(i * FW, D)
                pool.wait_ge(n_gamma, i + 1)
                v = y[:, t, c0:c0 + FW]
                pool.tensor_tensor(v, v, beta[:, c0:c0 + FW], ALU.add).then_inc(n_out_p, 1)

        @block.scalar
        def _(act):
            def split(n, g=0, per=TURN):
                s = n % RING
                act.wait_ge(landed[s], landed_at(n, g, per))
                if n >= RING:
                    act.wait_ge(s_used, g * per + (n - AHEAD))
                act.activation(w_hi[s][:, :], raw[s][:, :], ACT.Copy).then_inc(s_hi, 1)

            def x_high(q):
                for b in range(2):
                    act.wait_ge(xt_ps, 2 * q + b + 1)
                    k = 4 * q + 2 * b
                    act.activation(xt_hi[:, k:k + 2, :], bank[4 + q % 2 * 2 + b][:, :].rearrange(
                        "p (k t) -> p k t", k=2), ACT.Copy).then_inc(xt_h, 1)

            def a_high(i):
                for b in range(4):
                    act.wait_ge(a_ps, 4 * i + b + 1)
                    dst, src = a_block(i, 0, b)
                    act.activation(dst, src, ACT.Copy).then_inc(a_h, 1)

            x_high(0)
            for n in range(AHEAD):
                split(n)
            for i in range(PRO):
                if i < GC - 2 and i % 2 == 0:
                    x_high(i // 2 + 1)
                if i == GC + 4:
                    a_high(0)
                if i == MLP_K + 6:
                    act.wait_ge(hid_ps, 1)
                    act.activation(hid[:, 0].rearrange("p g n -> p (g n)"), bank[1][:, 2 * HD:2 * HD + 64],
                                   ACT.Silu).then_inc(hid_in, 1)
                if i == GATE0 + 1:
                    a_high(1)
                split(i + AHEAD)
            act.wait_ge(s_used, PRO)
            act.activation(gate_t[:, :], bank[0][:, 0:T], ACT.Copy).then_inc(gate_t_in, 1)
            act.wait_ge(hid_ps, 2)
            act.activation(hid[:, 1].rearrange("p g n -> p (g n)"), bank[3][:, 0:64],
                           ACT.Silu).then_inc(hid_in, 1)
            act.wait_ge(gates_ps, 1)
            act.activation(gates[:, :, :], bank[1][:, 0:T].rearrange("p (t c) -> p t c", t=TT)[:, :, P - NG:P],
                           ACT.Sigmoid).then_inc(gates_in, 1)

            def evacuate(dst, func, c, g, done):
                act.wait_ge(s_used, chunk_done(g, c))
                for t in range(TT):
                    act.activation(dst[:, t, :], bank[2 * PAIR[c] + t][:, :], func
                                   ).then_inc(done.sem, 1)

            with act.Fori(0, NKV) as g:
                for i in range(TURN):
                    if i == 3:
                        for b in range(2):
                            act.wait_ge(y_in.sem, y_in.at(g, b + 1))
                            act.activation(mix_hi[:, bass.ds(g * 4 + (12 + 2 * b), 2), :],
                                           conv[:, 2 * b:2 * b + 2, :], ACT.Copy).then_inc(y_hi.sem, 1)
                    if i == GC * (ZA + 1):
                        evacuate(tok_a, ACT.Silu, ZA, g, za_tok)
                    if i == GC * (ZA + 1) + 3:
                        act.wait_ge(z_ps.sem, z_ps.at(g, 1))
                        act.activation(z_t[:, 0:2, :], bank[6][:, :].rearrange("p (r t) -> p r t", r=2),
                                       ACT.Copy).then_inc(z_in.sem, 1)
                    if i == GC * (KV + 1):
                        evacuate(tok_b, ACT.Copy, KV, g, kv_tok)
                    if i == GC * (Q + 1):
                        evacuate(tok_a, ACT.Copy, Q, g, q_tok)
                    if i == GC * (Q + 1) + 3:
                        act.wait_ge(q_ps.sem, q_ps.at(g, 1))
                        act.activation(q_t[:, 0:2, :], bank[6][:, :].rearrange("p (r t) -> p r t", r=2),
                                       ACT.Copy).then_inc(q_in.sem, 1)
                    if i == I_CMP + 1:
                        act.wait_ge(sc_v.sem, sc_v.at(g, 3))
                        act.activation(ec[:, :, :, :], sc[:, :, :, :], ACT.Exp, scale=SCALE
                                       ).then_inc(ec_in.sem, 1)
                    for r in range(GQA):
                        if i == I_S + PERIOD * r:
                            act.wait_ge(neg_v.sem, neg_v.at(g, r + 1))
                            for t in range(TT):
                                for b in range(2):
                                    keys = (t + 1) * P
                                    last = act.activation(
                                        prob[:, t, b, 0:keys], bank[4 + t][:, b * keys:(b + 1) * keys],
                                        ACT.Exp, scale=SCALE, bias=s_neg[:, t, b:b + 1],
                                        accum_out=s_sum[:, t, b:b + 1])
                            last.then_inc(exp_in.sem, 1)
                        if i == I_T + PERIOD * r:
                            act.wait_ge(p_ps.sem, p_ps.at(g, 2 * r + 1))
                            act.activation(p_t0[:, :, 0:P], bank[6][:, 0:2 * P].rearrange(
                                "p (b q) -> p b q", b=2), ACT.Copy).then_inc(pt_a.sem, 1)
                            act.activation(pc_t[0:NC, :], bank[6][0:NC, 2 * P:4 * P], ACT.Copy
                                           ).then_inc(pt_a.sem, 1)
                        if i == I_V + PERIOD * r:
                            act.wait_ge(o_in.sem, o_in.at(g, r + 1))
                            act.activation(mix_hi[:, bass.ds(g * 4 + r, 1), :].rearrange("p a t -> p (a t)"),
                                           att[:, :], ACT.Copy).then_inc(o_hi.sem, 1)
                    if i == GC * (H + 1):
                        evacuate(tok_a, ACT.Copy, H, g, h_tok)
                    if i == GC * (ZC + 1):
                        evacuate(tok_b, ACT.Silu, ZC, g, zc_tok)
                    split(PRO + i + AHEAD, g)

            for i in range(GC):
                if i == 3:
                    for b in range(2):
                        act.wait_ge(y_in.sem, y_in.at(NKV, b + 1))
                        act.activation(mix_hi[:, KT - 4 + 2 * b:KT - 2 + 2 * b, :],
                                       conv[:, 2 * b:2 * b + 2, :], ACT.Copy).then_inc(y_hi.sem, 1)
                split(OUT0 + i + AHEAD)
            with act.Fori(1, NOUT - 1) as c:
                for i in range(GC):
                    split(OUT0 + i + AHEAD, c, GC)
            for i in range(GC - AHEAD):
                split(OUT0 + (NOUT - 1) * GC + i + AHEAD)

            def deviation(t):
                act.wait_ge(mv_in, t + 1)
                act.activation(std[:, t:t + 1], mv[:, t, 1:2], ACT.Sqrt, bias=eps[:, :]).then_inc(std_in, 1)

            deviation(0)
            for i in range(FIN):
                if i == FIN_T:
                    deviation(1)
                t, c0 = divmod(i * FW, D)
                v = y[:, t, c0:c0 + FW]
                act.wait_ge(shift_in, t + 1)
                act.activation(v, v, ACT.Identity, scale=rstd[:, t:t + 1], bias=shift[:, t:t + 1]
                               ).then_inc(n_scaled, 1)

        @block.vector
        def _(dve):
            def split(n, g=0, per=TURN, width=GK * W):
                s = n % RING
                dve.wait_ge(s_hi, g * per + (n + 1))
                dve.tensor_tensor(w_lo[s][:, 0:width], raw[s][:, 0:width], as_f32(w_hi[s][:, 0:width]),
                                  ALU.subtract).then_inc(s_lo, 1)

            def low(dst, src, high, done):
                dve.tensor_tensor(dst, src, as_f32(high), ALU.subtract).then_inc(done, 1)

            def x_low(q):
                for b in range(2):
                    dve.wait_ge(xt_h, 2 * q + b + 1)
                    k = 4 * q + 2 * b
                    low(xt_lo[:, k:k + 2, :], bank[4 + q % 2 * 2 + b][:, :].rearrange(
                        "p (k t) -> p k t", k=2), xt_hi[:, k:k + 2, :], xt_l)

            def a_low(i):
                for b in range(4):
                    dve.wait_ge(a_h, 4 * i + b + 1)
                    dst, src = a_block(i, 1, b)
                    low(dst, src, a_block(i, 0, b)[0], a_l)

            def a_tokens(i):
                for t in range(TT):
                    dve.wait_ge(s_used, (GC, GATE0)[i])
                    for h in range(2):
                        last = dve.tensor_tensor(
                            a_tok[:, i, h, t, :].rearrange("p (g d) -> p g d", g=NKV),
                            bank[2 * i + t][:, :].rearrange("p (g d) -> p g d", g=NKV),
                            pos_sb[:, i, h:h + 1, :].to_broadcast([P, NKV, HD]), ALU.add)
                        last.then_inc(a_in, 1)

            dve.memset(conv[:, :, :], 0.0).then_inc(cv.sem, 1)
            for t in range(TT):
                dve.memset(tok_b[:, t, :], 0.0).then_inc(zc_tok.sem, 1)
            x_low(0)
            for n in range(AHEAD):
                split(n)
            for i in range(PRO):
                if i < GC - 2 and i % 2 == 0:
                    x_low(i // 2 + 1)
                if i == GC:
                    dve.wait_ge(s_small, small)
                    a_tokens(0)
                if i == GC + 4:
                    a_low(0)
                if i == GC + 8:
                    dve.wait_ge(taps_ps, 1)
                    dve.tensor_copy(taps[:, :, :].rearrange("p k b -> p (k b)"), bank[6][:, 0:48]
                                    ).then_inc(taps_in, 1)
                if i == MLP_K + 4:
                    dve.wait_ge(s_used, i)
                    dve.tensor_copy(hid_4[:, 0].rearrange("p l e -> p (l e)"), bank[1][:, 0:2 * HD]
                                    ).then_inc(hid_4_in, 1)
                if i == MLP_K + 8:
                    dve.wait_ge(kc_ps, 1)
                    dve.tensor_copy(kc[:, :, :].rearrange("p g n -> p (g n)"), bank[1][:, 384:448]
                                    ).then_inc(kc_in, 1)
                if i == GATE0:
                    a_tokens(1)
                if i == GATE0 + 1:
                    a_low(1)
                if i == MLP_V + 4:
                    dve.wait_ge(s_used, i)
                    dve.tensor_copy(hid_4[:, 1].rearrange("p l e -> p (l e)"), bank[2][:, 0:2 * HD]
                                    ).then_inc(hid_4_in, 1)
                split(i + AHEAD)
            dve.wait_ge(vc_ps, 1)
            dve.tensor_copy(vc[0:NC, :, :], bank[7][0:NC, :].rearrange("p (g d) -> p g d", g=NKV)
                            ).then_inc(vc_in, 1)

            def gate(g):
                dve.wait_ge(s_used, chunk_done(g, -1))
                dve.wait_ge(zc_tok.sem, zc_tok.at(g, 0))
                for t in range(TT):
                    dve.tensor_tensor(tok_b[:, t, :], bank[4 + t][:, :], tok_b[:, t, :], ALU.mult
                                      ).then_inc(g_tok.sem, 1)

            def conv_out(g):
                dve.wait_ge(cv.sem, cv.at(g, 0))
                for b in range(2):
                    dve.wait_ge(g_ps.sem, g_ps.at(g, b + 1))
                    v = conv[:, 2 * b:2 * b + 2, :]
                    dve.tensor_tensor(v, bank[6 + b][:, :].rearrange("p (f t) -> p f t", f=2), v, ALU.mult
                                      ).then_inc(y_in.sem, 1)

            def conv_low(g, block0):
                for b in range(2):
                    dve.wait_ge(y_hi.sem, y_hi.at(g, b + 1))
                    at = bass.ds(block0 + 2 * b, 2)
                    low(mix_lo[:, at, :], conv[:, 2 * b:2 * b + 2, :], mix_hi[:, at, :], y_lo.sem)

            with dve.Fori(0, NKV) as g:
                for i in range(TURN):
                    if i == 0:
                        gate(g)
                    if i == 3:
                        conv_out(g)
                    if i == 4:
                        conv_low(g, g * 4 + 12)
                    if i == GC * (ZA + 1) + 3:
                        dve.wait_ge(z_ps.sem, z_ps.at(g, 2))
                        dve.tensor_copy(z_t[:, 2:4, :], bank[7][:, :].rearrange("p (r t) -> p r t", r=2)
                                        ).then_inc(z_in.sem, 1)
                    if i == GC * (KV + 1) + 3:
                        dve.wait_ge(k_ps.sem, k_ps.at(g, 1))
                        dve.tensor_copy(k_t[:, :, :], bank[6][:, :].rearrange("p (b t) -> p b t", b=2)
                                        ).then_inc(k_in.sem, 1)
                    if i == GC * (Q + 1) + 3:
                        dve.wait_ge(q_ps.sem, q_ps.at(g, 2))
                        dve.tensor_copy(q_t[:, 2:4, :], bank[7][:, :].rearrange("p (r t) -> p r t", r=2)
                                        ).then_inc(q_in.sem, 1)
                    if i == I_CMP:
                        dve.wait_ge(sc_ps.sem, sc_ps.at(g, 1))
                        scores = bank[7][:, 0:GQA * TT * 16].rearrange(
                            "p (r t n) -> p r t n", r=GQA, t=TT)[:, :, :, 0:NC]
                        for r in range(GQA):
                            last = dve.tensor_tensor(sc[:, r], scores[:, r], c_neg[:, :, :], ALU.add)
                        last.then_inc(sc_v.sem, 1)
                        dve.wait_ge(sc_v.sem, sc_v.at(g, 1))
                        flat = sc[:, :, :, :].rearrange("p r t n -> p (r t) n")
                        dve.tensor_reduce(c_max[:, :, :].rearrange("p r t -> p (r t)"), flat, AX.X, ALU.max
                                          ).then_inc(sc_v.sem, 1)
                        dve.wait_ge(sc_v.sem, sc_v.at(g, 2))
                        dve.tensor_tensor(flat, flat, over_keys(c_max), ALU.subtract).then_inc(sc_v.sem, 1)
                    if i == I_CMP + 2:
                        dve.wait_ge(ec_in.sem, ec_in.at(g, 1))
                        flat = ec[:, :, :, :].rearrange("p r t n -> p (r t) n")
                        dve.tensor_reduce(c_sum[:, :, :].rearrange("p r t -> p (r t)"), flat, AX.X, ALU.add
                                          ).then_inc(pc_v.sem, 1)
                        dve.wait_ge(pc_v.sem, pc_v.at(g, 1))
                        dve.reciprocal(c_rcp[:, :, :], c_sum[:, :, :]).then_inc(pc_v.sem, 1)
                        dve.wait_ge(pc_v.sem, pc_v.at(g, 2))
                        dve.wait_ge(group_in.sem, group_in.at(g, 4))
                        dve.tensor_tensor(c_fac[:, :, :], c_rcp[:, :, :],
                                          gates_g[:, :, :].rearrange("p t (r b) -> p r t b", b=3)[:, :, :, 0],
                                          ALU.mult).then_inc(pc_v.sem, 1)
                        dve.wait_ge(pc_v.sem, pc_v.at(g, 3))
                        dve.tensor_tensor(flat, flat, over_keys(c_fac), ALU.mult).then_inc(pc_v.sem, 1)
                        dve.wait_ge(pc_v.sem, pc_v.at(g, 4))
                        for r in range(GQA):
                            last = dve.tensor_tensor(ec[:, r], ec[:, r], c_ok[:, :, :], ALU.mult)
                        last.then_inc(pc_v.sem, 1)
                    for r in range(GQA):
                        if i == I_S + PERIOD * r:
                            for t in range(TT):
                                dve.wait_ge(s_ps.sem, s_ps.at(g, 2 * r + t + 1))
                                dve.tensor_reduce(s_max[:, t, :], bank[4 + t][:, 0:2 * (t + 1) * P].rearrange(
                                    "p (b k) -> p b k", b=2), AX.X, ALU.max).then_inc(mx_v.sem, 1)
                            dve.wait_ge(mx_v.sem, mx_v.at(g, 2 * r + 2))
                            dve.tensor_scalar(s_neg[:, :, :], s_max[:, :, :], -SCALE, None, ALU.mult
                                              ).then_inc(neg_v.sem, 1)
                        if i == I_S + PERIOD * r + 2:
                            dve.wait_ge(exp_in.sem, exp_in.at(g, r + 1))
                            dve.reciprocal(s_rcp[:, :, :], s_sum[:, :, :]).then_inc(rcp_v.sem, 1)
                            dve.wait_ge(rcp_v.sem, rcp_v.at(g, 2 * r + 1))
                            dve.tensor_tensor(s_fac[:, :, :], s_rcp[:, :, :],
                                              gates_g[:, :, 3 * r + 1:3 * r + 3], ALU.mult
                                              ).then_inc(rcp_v.sem, 1)
                            dve.wait_ge(rcp_v.sem, rcp_v.at(g, 2 * r + 2))
                            for t in range(TT):
                                for b in range(2):
                                    v = prob[:, t, b, 0:(t + 1) * P]
                                    last = dve.tensor_scalar(v, v, s_fac[:, t, b:b + 1], None, ALU.mult)
                                last.then_inc(p_in.sem, 1)
                        if i == I_T + PERIOD * r:
                            dve.wait_ge(p_ps.sem, p_ps.at(g, 2 * r + 2))
                            v = bank[7][:, :].rearrange("p (b k q) -> p b k q", b=2, k=2)
                            dve.tensor_copy(p_t0[:, :, P:T], v[:, :, 0, :]).then_inc(pt_v.sem, 1)
                            dve.tensor_copy(p_t1[:, :, :], v[:, :, 1, :]).then_inc(pt_v.sem, 1)
                        if i == I_V + PERIOD * r:
                            dve.wait_ge(o_ps.sem, o_ps.at(g, r + 1))
                            dve.tensor_tensor(att[:, :], bank[6][:, 0:T], z_t[:, r, :], ALU.mult
                                              ).then_inc(o_in.sem, 1)
                        if i == I_V + PERIOD * r + 1:
                            dve.wait_ge(o_hi.sem, o_hi.at(g, r + 1))
                            at = bass.ds(g * 4 + r, 1)
                            low(mix_lo[:, at, :].rearrange("p a t -> p (a t)"), att[:, :],
                                mix_hi[:, at, :].rearrange("p a t -> p (a t)"), o_lo.sem)
                    if i == GC * (CG + 1):
                        dve.wait_ge(s_used, chunk_done(g, CG))
                        dve.wait_ge(h_tok.sem, h_tok.at(g, 2))
                        for t in range(TT):
                            dve.tensor_tensor(tok_a[:, t, :], bank[2 * PAIR[CG] + t][:, :], tok_a[:, t, :],
                                              ALU.mult).then_inc(u_tok.sem, 1)
                    if i == I_U:
                        dve.wait_ge(group_in.sem, group_in.at(g, 4))
                        for tap in range(3):
                            for f in range(4):
                                u = bank[6 + f // 2][:, f % 2 * T:(f % 2 + 1) * T]
                                w = taps_g[:, 2 - tap, f:f + 1]
                                c = conv[:, f, tap:T]
                                if tap == 0:
                                    dve.wait_ge(u_ps.sem, u_ps.at(g, f // 2 + 1))
                                    dve.tensor_scalar(c, u, w, None, ALU.mult).then_inc(cv.sem, 1)
                                else:
                                    dve.wait_ge(cv.sem, cv.at(g, 4 * tap + f - 3))
                                    dve.scalar_tensor_tensor(out=c, in0=u[:, 0:T - tap], scalar=w, in1=c,
                                                             op0=ALU.mult, op1=ALU.add).then_inc(cv.sem, 1)
                    split(PRO + i + AHEAD, g)

            def tile_sums(c, b, t):
                dve.scalar_tensor_tensor(out=y[:, t, bass.ds(c * W, W)], in0=x_res[b][:, t, :],
                                         scalar=ALPHA, in1=bank[2 * (1 - b) + t][:, :],
                                         op0=ALU.mult, op1=ALU.add).then_inc(y_sum, 1)

            def tile_stats(c, t, sums):
                dve.wait_ge(y_sum, sums)
                st = stats[:, t, bass.ds(c, 1), :].rearrange("p a s -> p (a s)")
                dve.bn_stats(st, y[:, t, bass.ds(c * W, W)]).then_inc(y_stat, 1)

            def chunk_sums(c, b, loads, done, before):
                dve.wait_ge(s_used, done)
                dve.wait_ge(res_in[b], loads)
                for t in range(TT):
                    tile_sums(c, b, t)
                for t in range(TT):
                    tile_stats(c, t, before + (t + 1))

            for i in range(GC):
                if i == 0:
                    gate(NKV)
                if i == 3:
                    conv_out(NKV)
                if i == 4:
                    conv_low(NKV, KT - 4)
                    dve.wait_ge(y_lo.sem, y_lo.at(NKV, 2))
                    dve.memset(eps[:, :], EPS).then_inc(y_sum, 4)
                split(OUT0 + i + AHEAD)
            with dve.Fori(0, NOUT // 2 - 1) as c2:
                for b in range(2):
                    chunk_sums(c2 * 2 + b, b, c2 * 16 + 16, c2 * (2 * GC) + (OUT0 + (b + 1) * GC),
                               c2 * 4 + (4 + 2 * b))
                    for i in range(GC):
                        split(OUT0 + (b + 1) * GC + i + AHEAD, c2, 2 * GC)
            c = NOUT - 2
            chunk_sums(c, 0, c // 2 * 16 + 16, OUT0 + (c + 1) * GC, 4 + 2 * c)
            for i in range(GC - AHEAD):
                split(OUT0 + (NOUT - 1) * GC + i + AHEAD)

            def mean_var(t):
                tile_sums(NOUT - 1, 1, t)
                tile_stats(NOUT - 1, t, 4 + 2 * (NOUT - 1) + t + 1)
                dve.wait_ge(y_stat, 2 * NOUT - 1 + t)
                dve.bn_aggr(mv[:, t, :], stats[:, t, :, :].rearrange("p c s -> p (c s)")
                            ).then_inc(mv_in, 1)

            def scale_shift(t):
                dve.wait_ge(std_in, t + 1)
                dve.reciprocal(rstd[:, t:t + 1], std[:, t:t + 1]).then_inc(rstd_in, 1)
                dve.wait_ge(rstd_in, t + 1)
                dve.scalar_tensor_tensor(out=shift[:, t:t + 1], in0=mv[:, t, 0:1], scalar=-1.0,
                                         in1=rstd[:, t:t + 1], op0=ALU.mult, op1=ALU.mult
                                         ).then_inc(shift_in, 1)

            dve.wait_ge(out_tile0, 1)
            dve.wait_ge(res_in[1], NOUT // 2 * 16)
            mean_var(0)
            scale_shift(0)
            dve.wait_ge(norm_in, 32)
            for i in range(FIN):
                if i == FIN_T - 2:
                    dve.wait_ge(s_used, LAST)
                    mean_var(1)
                if i == FIN_T - 1:
                    scale_shift(1)
                t, c0 = divmod(i * FW, D)
                v = y[:, t, c0:c0 + FW]
                dve.wait_ge(n_scaled, i + 1)
                dve.tensor_tensor(v, v, gamma[:, c0:c0 + FW], ALU.mult).then_inc(n_gamma, 1)
                if i in FIN_DVE:
                    dve.wait_ge(n_gamma, i + 1)
                    dve.tensor_tensor(v, v, beta[:, c0:c0 + FW], ALU.add).then_inc(n_out_v, 1)

        @block.tensor
        def _(pe):
            def granule(s, hi, lo, k0, pair, width, tiles, first, last, tokens=range(TT)):
                for k in range(tiles):
                    wh = w_hi[s][:, k * width:(k + 1) * width]
                    wl = w_lo[s][:, k * width:(k + 1) * width]
                    for t in tokens:
                        xh, xl = (m[:, k0 + k, t * P:(t + 1) * P] for m in (hi, lo))
                        acc = bank[2 * pair + t][:, 0:width]
                        pe.matmul(acc, xh, wl, start=first and k == 0, stop=False)
                        pe.matmul(acc, xh, wh, start=False, stop=False)
                        mm = pe.matmul(acc, xl, wh, start=False, stop=last and k == tiles - 1)
                return mm

            def transpose(dst, src):
                rows = src.shape[0]
                return pe.transpose(dst, src, ident[0:rows, 0:rows])

            def x_transposes(q):
                pe.wait_ge(x_in[q], 16)
                for b in range(2):
                    if q >= 2:
                        pe.wait_ge(xt_l, 2 * (q - 2) + b + 1)
                    for k in range(2):
                        kt = 4 * q + 2 * b + k
                        for t in range(TT):
                            last = transpose(bank[4 + q % 2 * 2 + b][:, k * T + t * P:k * T + (t + 1) * P],
                                             x_tok[:, t, kt * P:(kt + 1) * P])
                    last.then_inc(xt_ps, 1)

            def a_transposes(i):
                pe.wait_ge(a_in, 4 * i + 4)
                for b in range(4):
                    if i == 0:
                        pe.wait_ge(xt_l, 2 * XP)
                    else:
                        pe.wait_ge(taps_in, 1)
                    h = b // 2
                    for gg in range(2):
                        g = b % 2 * 2 + gg
                        for t in range(TT):
                            last = transpose(bank[4 + b][:, gg * T + t * P:gg * T + (t + 1) * P],
                                             a_tok[:, i, h, t, g * HD:(g + 1) * HD])
                    last.then_inc(a_ps, 1)

            def chunk_granules(base, g, per, hi, lo, pair, steps):
                for j in range(GC):
                    steps(j)
                    n = base + j
                    if base == GC and n >= MLP_K:
                        n += 4
                    pe.wait_ge(s_lo, g * per + (n + 1))
                    granule(n % RING, hi, lo, GK * j, pair, W, GK, j == 0, j == GC - 1).then_inc(s_used, 1)

            pe.wait_ge(s_const, 5)
            x_transposes(0)

            def chunk0_steps(j):
                if j < GC - 2 and j % 2 == 0:
                    x_transposes(j // 2 + 1)
                pe.wait_ge(xt_l, j + 1)

            def mlp(i, j, acc):
                n = (MLP_K, MLP_V)[i] + j
                pe.wait_ge(s_lo, n + 1)
                pe.wait_ge(a_l, 4 * i + 4)
                for k in range(8):
                    h, at = divmod(8 * j + k, DC)
                    tokens = a_t[:, i, h].rearrange("p l g t -> p l (g t)")[:, :, at:NKV * T:DC]
                    mm = pe.matmul(acc.rearrange("p (l e) -> p l e", l=2), tokens,
                                   parts[n % RING][:, :, k * HD:(k + 1) * HD],
                                   start=j == 0 and k == 0, stop=j == 3 and k == 7)
                mm.then_inc(s_used, 1)

            def sum_parts(i, acc):
                pe.wait_ge(hid_4_in, i + 1)
                pe.matmul(acc, hid_4[:, i, 0, :], fold[:, :], start=True, stop=False)
                pe.matmul(acc, hid_4[:, i, 1, :], fold[:, :], start=False, stop=True).then_inc(hid_ps, 1)

            def chunk1_steps(j):
                i = GC + j + (4 if j >= MLP_K - GC else 0)
                if i == GC + 4:
                    a_transposes(0)
                if i == GC + 8:
                    pe.wait_ge(s_small, small)
                    pe.wait_ge(a_l, 4)
                    transpose(bank[6][:, 0:48], conv_rows[:, :]).then_inc(taps_ps, 1)
                if i == MLP_K + 4:
                    pe.wait_ge(a_pad, 4)
                    for m in range(4):
                        mlp(0, m, bank[1][:, 0:2 * HD])
                if i == MLP_K + 6:
                    pe.wait_ge(s_const, 7)
                    sum_parts(0, bank[1][:, 2 * HD:2 * HD + 64])
                if i == MLP_K + 8:
                    pe.wait_ge(hid_in, 1)
                    pe.matmul(bank[1][:, 384:448], w2_sb[:, 0, :], hid[:, 0].rearrange("p g n -> p (g n)"),
                              start=True, stop=True).then_inc(kc_ps, 1)

            def gate_granule(n):
                pe.wait_ge(s_lo, n + 1)
                j = n - GATE0 - (4 if n >= MLP_V else 0)
                for k in range(8):
                    wh, wl = (m[n % RING][:, k * P:(k + 1) * P] for m in (w_hi, w_lo))
                    xh, xl = (m[:, 8 * j + k, :] for m in (xt_hi, xt_lo))
                    acc = bank[0][:, 0:T]
                    pe.matmul(acc, wh, xl, start=j == 0 and k == 0, stop=False)
                    pe.matmul(acc, wh, xh, start=False, stop=False)
                    mm = pe.matmul(acc, wl, xh, start=False, stop=j == 3 and k == 7)
                mm.then_inc(s_used, 1)

            chunk_granules(0, 0, 0, xt_hi, xt_lo, 0, chunk0_steps)
            chunk_granules(GC, 0, 0, xt_hi, xt_lo, 1, chunk1_steps)
            gate_granule(GATE0)
            a_transposes(1)
            gate_granule(GATE0 + 1)
            gate_granule(GATE0 + 2)
            for m in range(4):
                mlp(1, m, bank[2][:, 0:2 * HD])
            gate_granule(MLP_V + 4)
            sum_parts(1, bank[3][:, 0:64])
            pe.wait_ge(gate_t_in, 1)
            for t in range(TT):
                last = transpose(bank[1][:, t * P:(t + 1) * P], gate_t[:, t * P:(t + 1) * P])
            last.then_inc(gates_ps, 1)
            pe.wait_ge(hid_in, 2)
            for g in range(NKV):
                mm = pe.matmul(bank[7][0:NC, g * HD:(g + 1) * HD], hid[:, 1, g, 0:NC], w2_sb[:, 1, :],
                               start=True, stop=True)
            mm.then_inc(vc_ps, 1)

            def gate_transposes(g):
                pe.wait_ge(cv.sem, cv.at(g, 0))
                pe.wait_ge(g_tok.sem, g_tok.at(g, 2))
                for b in range(2):
                    for f in range(2):
                        for t in range(TT):
                            last = transpose(bank[6 + b][:, f * T + t * P:f * T + (t + 1) * P],
                                             tok_b[:, t, (2 * b + f) * P:(2 * b + f + 1) * P])
                    last.then_inc(g_ps.sem, 1)

            def heads_transposes(done):
                for b in range(2):
                    for f in range(2):
                        for t in range(TT):
                            last = transpose(bank[6 + b][:, f * T + t * P:f * T + (t + 1) * P],
                                             tok_a[:, t, (2 * b + f) * P:(2 * b + f + 1) * P])
                    last.then_inc(done.sem, 1)

            def group_steps(g, i):
                if i == 3:
                    gate_transposes(g)
                if i == GC * KV:
                    pe.wait_ge(gates_in, 1)
                if i == GC * (ZA + 1) + 3:
                    pe.wait_ge(za_tok.sem, za_tok.at(g, 2))
                    pe.wait_ge(y_in.sem, y_in.at(g, 2))
                    heads_transposes(z_ps)
                if i == GC * (KV + 1) + 3:
                    pe.wait_ge(kv_tok.sem, kv_tok.at(g, 2))
                    pe.wait_ge(z_in.sem, z_in.at(g, 2))
                    for b in range(2):
                        for t in range(TT):
                            last = transpose(bank[6][:, b * T + t * P:b * T + (t + 1) * P],
                                             tok_b[:, t, 2 * b * P:(2 * b + 1) * P])
                    last.then_inc(k_ps.sem, 1)
                if i == GC * (Q + 1) + 3:
                    pe.wait_ge(q_tok.sem, q_tok.at(g, 2))
                    pe.wait_ge(k_in.sem, k_in.at(g, 1))
                    heads_transposes(q_ps)
                if i == I_CMP:
                    pe.wait_ge(q_in.sem, q_in.at(g, 2))
                    pe.wait_ge(group_in.sem, group_in.at(g, 4))
                    for r in range(GQA):
                        for t in range(TT):
                            c0 = (r * TT + t) * 16
                            mm = pe.matmul(bank[7][:, c0:c0 + NC], q_t[:, r, t * P:(t + 1) * P], kc_g[:, 0:NC],
                                           start=True, stop=True)
                    mm.then_inc(sc_ps.sem, 1)
                for r in range(GQA):
                    if i == I_S + PERIOD * r:
                        if r:
                            pe.wait_ge(exp_in.sem, exp_in.at(g, r))
                        else:
                            pe.wait_ge(g_tok.sem, g_tok.at(g, 2))
                        for t in range(TT):
                            keys = (t + 1) * P
                            for b in range(2):
                                acc = bank[4 + t][:, b * keys:(b + 1) * keys]
                                pe.matmul(acc, q_t[:, r, t * P:(t + 1) * P], k_t[:, b, 0:keys],
                                          start=True, stop=False)
                                mm = pe.matmul(acc[:, t * P:keys], ident_b[:, :], causal[:, :],
                                               start=False, stop=True)
                            mm.then_inc(s_ps.sem, 1)
                    if i == I_T + PERIOD * r:
                        pe.wait_ge(p_in.sem, p_in.at(g, 2 * r + 2))
                        if r == 0:
                            pe.wait_ge(pc_v.sem, pc_v.at(g, 5))
                        else:
                            pe.wait_ge(o_in.sem, o_in.at(g, r))
                        for b in range(2):
                            transpose(bank[6][:, b * P:(b + 1) * P], prob[:, 0, b, 0:P])
                        for t in range(TT):
                            last = transpose(bank[6][0:NC, (2 + t) * P:(3 + t) * P], ec[:, r, t, :])
                        last.then_inc(p_ps.sem, 1)
                        for b in range(2):
                            for k in range(TT):
                                c0 = (2 * b + k) * P
                                last = transpose(bank[7][:, c0:c0 + P], prob[:, 1, b, k * P:(k + 1) * P])
                        last.then_inc(p_ps.sem, 1)
                    if i == I_V + PERIOD * r:
                        pe.wait_ge(pt_a.sem, pt_a.at(g, 2 * r + 2))
                        pe.wait_ge(pt_v.sem, pt_v.at(g, 2 * r + 2))
                        acc = bank[6][:, 0:T]
                        pe.matmul(acc, vc_g[0:NC, :], pc_t[0:NC, :], start=True, stop=False)
                        for b in range(2):
                            v = tok_b[:, :, (2 * b + 1) * P:(2 * b + 2) * P]
                            pe.matmul(acc, v[:, 0, :], p_t0[:, b, :], start=False, stop=False)
                            mm = pe.matmul(acc[:, P:T], v[:, 1, :], p_t1[:, b, :], start=False, stop=b == 1)
                        mm.then_inc(o_ps.sem, 1)
                if i == GC * ZC:
                    pe.wait_ge(h_tok.sem, h_tok.at(g, 2))
                if i == I_U:
                    pe.wait_ge(u_tok.sem, u_tok.at(g, 2))
                    pe.wait_ge(o_in.sem, o_in.at(g, GQA))
                    heads_transposes(u_ps)

            pe.wait_ge(vc_in, 1)
            with pe.Fori(0, NKV) as g:
                for c in range(CH):
                    chunk_granules(PRO + c * GC, g, TURN, xt_hi, xt_lo, PAIR[c],
                                   lambda j, c=c: group_steps(g, c * GC + j))

            def first_steps(j):
                if j == 0:
                    pe.wait_ge(zc_tok.sem, zc_tok.at(NKV, 0))
                if j == 3:
                    gate_transposes(NKV)
                if j == 14:
                    pe.wait_ge(y_lo.sem, y_lo.at(NKV, 2))

            def no_steps(j):
                pass

            chunk_granules(OUT0, 0, 2 * GC, mix_hi, mix_lo, 1, first_steps)
            chunk_granules(OUT0 + GC, 0, 2 * GC, mix_hi, mix_lo, 0, no_steps)
            with pe.Fori(1, NOUT // 2 - 1) as c2:
                for b in range(2):
                    pe.wait_ge(y_sum, c2 * 4 + (2 * b + 2))
                    chunk_granules(OUT0 + b * GC, c2, 2 * GC, mix_hi, mix_lo, 1 - b, no_steps)
            pe.wait_ge(y_sum, 2 * NOUT - 2)
            chunk_granules(LAST - 2 * GC, 0, 0, mix_hi, mix_lo, 1, no_steps)
            pe.wait_ge(y_sum, 2 * NOUT)
            for j in range(GC - RING):
                n = LAST - GC + j
                pe.wait_ge(s_lo, n + 1)
                granule(n % RING, mix_hi, mix_lo, GK * j, 0, W, GK, j == 0, False).then_inc(s_used, 1)
            for t in range(TT):
                for j in range(GC - RING, GC):
                    n = LAST - GC + j
                    if t == 0:
                        pe.wait_ge(s_lo, n + 1)
                    mm = granule(n % RING, mix_hi, mix_lo, GK * j, 0, W, GK, False, j == GC - 1, (t,))
                    if t == 1:
                        mm.then_inc(s_used, 1)
                    elif j == GC - 1:
                        mm.then_inc(out_tile0, 1)


NAMES = ["x", "w_in", "conv_w", "cmp_pos_k", "cmp_w1_k", "cmp_w2_k", "cmp_pos_v", "cmp_w1_v",
         "cmp_w2_v", "w_out", "ln_g", "ln_b"]


def kernel(**inputs):
    import concourse.bacc as bacc
    from concourse.bass_utils import run_bass_kernel_spmd as run

    nc = bacc.Bacc("TRN2", target_bir_lowering=False, num_devices=1, dynamic_dma_scratch_size=8192)
    arrays, args = {}, []
    for name in NAMES:
        a = np.ascontiguousarray(inputs[name])
        arrays[f"in_{name}"] = a
        args.append(nc.dram_tensor(f"in_{name}", a.shape, mybir.dt.from_np(a.dtype),
                                   kind="ExternalInput").ap())
    o = nc.dram_tensor("out_y", (1, T, D), F32, kind="ExternalOutput").ap()
    build(nc, *args, o)
    return run(nc, [arrays], core_ids=[0]).results[0]["out_y"]
```

```python
from contextlib import ExitStack

import numpy as np

import concourse.bass as bass
from concourse import mybir

F32 = mybir.dt.float32
F32R = mybir.dt.float32r
BF16 = mybir.dt.bfloat16
ALU = mybir.AluOpType
ACT = mybir.ActivationFunctionType
AX = mybir.AxisListType

P = 128
D = 4096
T = 256
TT = T // P
KT = D // P
W = 512
WC = 2048
HD = 128
NKV = 4
GQA = 4
WKV = NKV * HD
LC, DC = 32, 16
NC = T // DC - LC // DC + 1
SCALE = float(HD) ** -0.5
ALPHA = 2.0 ** 0.25
EPS = 1e-5
NEG = -1e30

C_H, C_BG, C_CG, C_ZC, C_Q = (WC * i for i in range(5))
C_KCMP = 5 * WC
C_VCMP = C_KCMP + WKV
C_KV = C_VCMP + WKV
C_ZA = C_KV + 4 * WKV
C_GATE = C_ZA + WC
NG = 48
GW = P // 2

GK = 2
GC = KT // GK
RING = 4
AHEAD = RING - 1
MLP_K = GC + 10
GATE0 = 2 * GC + 4
MLP_V = GATE0 + 3
PRO = GATE0 + 8
XP = GC
XA = 2
XS = 8
CH = 7
TURN = CH * GC
OUT0 = PRO + NKV * TURN
NOUT = D // W
LAST = OUT0 + NOUT * GC
assert TURN % RING == 0 and GC % RING == 0

ZA, KV, Q, H, CG, ZC, BG = range(CH)
PAIR = (1, 0, 1, 0, 1, 0, 2)
I_S, I_T, I_V, PERIOD = 57, 60, 66, 10
I_U = CH * GC - 15
TQ = 32
NQ = P // TQ
CP = 16
COLS = {ZA: C_ZA, Q: C_Q, H: C_H, CG: C_CG, ZC: C_ZC, BG: C_BG}

FIN = TT * NOUT
FIN_P = (1, 4, 6)
NP, NV = len(FIN_P), NOUT - len(FIN_P)
FB = 6
STORES = ((0, 2, 1, 3, 4, 5, 6, 7), (0, 2, 3, 1, 5, 4, 7, 6))
LOW = 32
RA = LOW + 2


def by_pool(i):
    return i % NOUT in FIN_P


def finished(i):
    return sum(1 for k in range(i + 1) if by_pool(k) == by_pool(i))


def is_gate(n):
    return GATE0 <= n < MLP_V or MLP_V + 4 <= n < PRO


class Signal:

    def __init__(self, sem, per=0, before=0):
        self.sem, self.per, self.before = sem, per, before

    def at(self, g, k):
        return g * self.per + (self.before + k)


def chunk_done(g, c):
    return g * TURN + (PRO + GC * (c + 1))


def landed_at(n, g=0, per=TURN):
    first, twice = PRO + KV * GC, GC // RING
    if n >= OUT0:
        extra, again = NKV * twice, 0
    else:
        extra, again = min(max((n - first) // RING + 1, 0), twice), twice
    return g * (16 * (per // RING + again)) + 16 * (n // RING + 1 + extra)


def build(nc, x, w_in, conv_w, pos_k, w1_k, w2_k, pos_v, w1_v, w2_v, w_out, ln_g, ln_b, out):
    x, out = x[0], out[0]
    w_in, conv_w, w_out = w_in[0], conv_w[0], w_out[0]
    pos, w1, w2 = (pos_k[0], pos_v[0]), (w1_k[0], w1_v[0]), (w2_k[0], w2_v[0])

    with ExitStack() as ctx:
        top = [(nc.sbuf_base + 31) // 32 * 32]

        def region(kib):
            at = top[0]
            top[0] += int(kib * 1024)
            return at

        def place(name, shape, dt, at):
            return nc.alloc_sbuf_tensor_at(name, shape, dt, offset=at)

        def own(name, shape, dt):
            size = int(np.prod(shape[1:])) * (2 if dt == BF16 else 4)
            return place(name, shape, dt, region((size + 31) // 32 * 32 / 1024))

        r_x = region(64)
        xt_hi = place("xt_hi", [P, KT, T], F32R, r_x)
        xt_lo = place("xt_lo", [P, KT, T], F32R, r_x + 32 * 1024)
        y = place("y", [P, TT, D], F32, r_x)
        gamma = place("gamma", [P, D], F32, r_x + 32 * 1024)
        affine = place("affine", [RA, D], F32R, r_x + 48 * 1024)

        r_m = region(64)
        mix_hi = place("mix_hi", [P, KT, T], F32R, r_m)
        mix_lo = place("mix_lo", [P, KT, T], F32R, r_m + 32 * 1024)
        x_tok = place("x_tok", [P, TT, D], F32, r_m)
        a_tok = place("a_tok", [P, 2, 2, TT, W], F32, r_m)
        a_t = place("a_t", [P, 2, 2, 2, NKV, T], F32R, r_m + 32 * 1024)

        raw = [own(f"raw{i}", [P, GK * W], F32) for i in range(RING)]
        parts = [own(f"parts{i}", [P, 2, GK * W], F32R) for i in range(RING)]
        w_hi, w_lo = ([w[:, i, :] for w in parts] for i in range(2))

        r_s = top[0]
        tok_a = own("tok_a", [P, TT, W], F32)
        tok_b = own("tok_b", [P, TT, W], F32)
        v_parts = place("v_parts", [P, TT, W], F32R, r_s + TT * W * 4)
        r_k = top[0]
        keys = own("keys", [P, 2, CP + T], F32)
        keys_lo = place("keys_lo", [P, 2, CP + T], F32R, r_k)
        keys_hi = own("keys_hi", [P, 2, CP + T], F32R)
        r_q = top[0]
        q_t = own("q_t", [P, GQA, T], F32)
        q_lo = place("q_lo", [P, GQA, T], F32R, r_q)
        q_hi = own("q_hi", [P, GQA, T], F32R)
        z_t = own("z_t", [P, GQA, T], F32)
        r_prob = top[0]
        prob = own("prob", [P, 2, 3, P], F32)
        r_p = top[0]
        p_t = own("p_t", [P, 2, 3, P], F32)
        p_lo = place("p_lo", [P, 2, 3, P], F32R, r_p)
        p_hi = own("p_hi", [P, 2, 2, P], F32R)
        pc_s = own("pc_s", [P, T], F32R)
        pc_t = place("pc_t", [P, T], F32, top[0] - T * 4)
        conv = place("conv", [P, 4, T], F32, r_prob)
        att = own("att", [P, T], F32)
        ident = own("ident", [P, P], F32)
        causal = own("causal", [P, P], F32)
        c_neg = own("c_neg", [P, TT, NC], F32)
        c_ok = own("c_ok", [P, TT, NC], F32)
        taps = own("taps", [P, 3, 16], F32)
        taps_g = own("taps_g", [P, 3, 4], F32)
        gates = own("gates", [P, TT, NG], F32)
        gates_g = own("gates_g", [P, TT, GQA * 3], F32)
        kc = own("kc", [P, NKV, DC], F32)
        vc = own("vc", [P, NKV, HD], F32R)
        vc_g = own("vc_g", [P, HD], F32R)
        sc = own("sc", [P, TT, NC], F32)
        ec = own("ec", [P, TT, TQ], F32)
        c_max = own("c_max", [P, TT], F32)
        s_max = own("s_max", [P, TT, 2], F32)
        s_neg = own("s_neg", [P, TT, 2], F32)
        s_sum = own("s_sum", [P, TT, 3], F32)
        s_rcp = own("s_rcp", [P, TT, 3], F32)
        s_fac = own("s_fac", [P, TT, 3], F32)
        assert top[0] <= nc.sbuf_usable_end, (top[0], nc.sbuf_usable_end)

        conv_rows = place("conv_rows", [48, P], F32, r_s + 8 * 1024)
        pos_sb = place("pos_sb", [P, 2, 2, HD], F32, r_s + 9 * 1024)
        w2_sb = place("w2_sb", [P, 2, HD], F32, r_s + 11 * 1024)
        hid = place("hid", [P, 2, NKV, DC], F32, r_s + 12 * 1024)
        hid_4 = place("hid_4", [P, 2, 2, HD], F32, r_s)
        gate_t = place("gate_t", [P, T], F32, r_s + 2048)
        fold = place("fold", [P, P // 2], F32, r_s + 3072)
        x_res = [place(f"x_res{i}", [P, TT, W], F32, r_s + 4096 * i) for i in range(2)]
        stats = place("stats", [P, TT, NOUT, 6], F32, r_s + 8192)
        mv = place("mv", [P, TT, 2], F32, r_s + 9 * 1024)
        eps = place("eps", [P, 1], F32, r_s + 9 * 1024 + 64)
        std = place("std", [P, TT], F32, r_s + 9 * 1024 + 128)
        rstd = place("rstd", [P, TT], F32, r_s + 9 * 1024 + 192)
        shift = place("shift", [P, TT], F32, r_s + 9 * 1024 + 256)
        terms = place("terms", [P, TT, RA], F32, r_s + 9 * 1024 + 320)
        affine_raw = place("affine_raw", [RA, D // 2], F32, r_s + 10 * 1024)
        offset = place("offset", [P, NP, W], F32, r_s + 18 * 1024)
        terms_t = place("terms_t", [RA, TT, P], F32R, r_s + 24 * 1024)

        bank = [ctx.enter_context(nc.psum_tensor(f"bank{i}", [P, W], F32)) for i in range(8)]

        def sem(name):
            return ctx.enter_context(nc.semaphore(name))

        landed = [sem(f"landed{i}") for i in range(RING)]
        s_hi = sem("s_hi")
        s_lo = sem("s_lo")
        s_used = sem("s_used")
        s_const = sem("s_const")
        s_pool = sem("s_pool")
        s_small = sem("s_small")
        x_in = [sem(f"x_in{i}") for i in range(XS)]
        xt_ps, xt_h, xt_l = sem("xt_ps"), sem("xt_h"), sem("xt_l")
        taps_ps, taps_in = sem("taps_ps"), sem("taps_in")
        a_in = sem("a_in")
        a_ps, a_h, a_l = sem("a_ps"), sem("a_h"), sem("a_l")
        a_pad = sem("a_pad")
        ec_0 = sem("ec_0")
        hid_4_in, hid_ps, hid_in = sem("hid_4_in"), sem("hid_ps"), sem("hid_in")
        gate_t_in, gates_ps, gates_in = sem("gate_t_in"), sem("gates_ps"), sem("gates_in")
        kc_ps, kc_in, vc_ps, vc_in = sem("kc_ps"), sem("kc_in"), sem("vc_ps"), sem("vc_in")
        vc_0, vc_h = sem("vc_0"), sem("vc_h")
        gate_sum_1, gate_sum = sem("gate_sum_1"), sem("gate_sum")

        group_in = Signal(sem("group_in"), 5)
        g_tok = Signal(sem("g_tok"), 2)
        g_in = Signal(sem("g_in"), 1)
        y_in = Signal(sem("y_in"), 2)
        y_hi = Signal(sem("y_hi"), 2)
        y_lo = Signal(sem("y_lo"), 2)
        za_tok = Signal(sem("za_tok"), 2)
        z_in = Signal(sem("z_in"), 1)
        kv_tok = Signal(sem("kv_tok"), 2)
        k_in = Signal(sem("k_in"), 1)
        k_hi, k_lo = Signal(sem("k_hi"), 1), Signal(sem("k_lo"), 1)
        v_h, v_l = Signal(sem("v_h"), 1), Signal(sem("v_l"), 1)
        q_tok = Signal(sem("q_tok"), 2)
        q_in = Signal(sem("q_in"), 1)
        q_h, q_l = Signal(sem("q_h"), 1), Signal(sem("q_l"), 1)
        s_ps = Signal(sem("s_ps"), 2 * GQA)
        mask_v = Signal(sem("mask_v"), 5 * GQA)
        mx_v = Signal(sem("mx_v"), 4 * GQA)
        neg_v = Signal(sem("neg_v"), 2 * GQA)
        exp_in = Signal(sem("exp_in"), GQA)
        rcp_v = Signal(sem("rcp_v"), 3 * GQA)
        p_in = Signal(sem("p_in"), 2 * GQA)
        pt_h, pt_l = Signal(sem("pt_h"), 3 * GQA), Signal(sem("pt_l"), 2 * GQA)
        pt_in = Signal(sem("pt_in"), GQA)
        o_ps = Signal(sem("o_ps"), GQA)
        o_in = Signal(sem("o_in"), GQA)
        o_hi = Signal(sem("o_hi"), GQA)
        o_lo = Signal(sem("o_lo"), GQA)
        h_tok = Signal(sem("h_tok"), 2)
        u_tok = Signal(sem("u_tok"), 2)
        zc_tok = Signal(sem("zc_tok"), 2, 2)
        u_in = Signal(sem("u_in"), 1)
        cv = Signal(sem("cv"), 12, 1)

        res_in = [sem(f"res_in{i}") for i in range(2)]
        norm_in = sem("norm_in")
        y_sum = sem("y_sum")
        y_stat = sem("y_stat")
        out_tile0 = sem("out_tile0")
        mv_in, std_in = sem("mv_in"), sem("std_in")
        rstd_in, shift_in = sem("rstd_in"), sem("shift_in")
        affine_zero, affine_raw_in = sem("affine_zero"), sem("affine_raw_in")
        affine_hi, affine_lo = sem("affine_hi"), sem("affine_lo")
        y_gamma = sem("y_gamma")
        terms_0 = sem("terms_0")
        terms_in, terms_ps, terms_t_in = sem("terms_in"), sem("terms_ps"), sem("terms_t_in")
        offset_ps = sem("offset_ps")
        offset_in = sem("offset_in")
        scaled = sem("scaled")
        n_out_v, n_out_p = sem("n_out_v"), sem("n_out_p")
        stored = sem("stored")
        small = 16 * (1 + 2 * (P // DC + 1))

        block = ctx.enter_context(nc.Block())

        def as_f32(ap):
            return ap.bitcast(F32)

        def a_block(i, part, b):
            h, g0 = b // 2, b % 2 * 2
            src = bank[4 + b][:, :].rearrange("p (g t) -> p g t", g=2)
            return a_t[:, i, h, part, g0:g0 + 2, 0:T - h * DC], src[:, :, h * DC:T]

        def scores_of(t, b):
            if t == 0:
                at = b * (CP + P) + CP
                return bank[4][:, at:at + P]
            return bank[5][:, CP:CP + T] if b == 0 else bank[7][:, 0:T]

        def v_strips(tok, t, v):
            return tok[:, t, :].rearrange("p (b v d) -> p b v d", b=2, v=2)[:, :, v, :]

        @block.sync
        def _(sp):
            def load(slot, src, shape):
                k, c = shape
                dst = raw[slot][:, 0:k * c].rearrange("p (k c) -> p k c", k=k)
                sp.dma_start(dst, src).then_inc(landed[slot], 16)

            def rows(w, r0, n, c0, width):
                return w[bass.ds(r0, n * P), bass.ds(c0, width)].rearrange("(k p) c -> p k c", p=P)

            def first_loads(n):
                if n < GC:
                    load(n % RING, rows(w_in, n * GK * P, GK, C_KCMP, W), (GK, W))
                elif MLP_K <= n < MLP_K + 4:
                    load(n % RING, rows(w1[0], (n - MLP_K) * 8 * HD, 8, 0, HD), (8, HD))
                elif n < GATE0:
                    j = n - GC - (4 if n >= MLP_K else 0)
                    load(n % RING, rows(w_in, j * GK * P, GK, C_VCMP, W), (GK, W))
                elif MLP_V <= n < MLP_V + 4:
                    load(n % RING, rows(w1[1], (n - MLP_V) * 8 * HD, 8, 0, HD), (8, HD))
                else:
                    j = n - GATE0 - (4 if n >= MLP_V else 0)
                    load(n % RING, rows(w_in, j * 8 * P, 8, C_GATE + NG - P, P), (8, P))

            def x_piece(q):
                cols = slice(q * D // XP, (q + 1) * D // XP)
                sp.dma_start(x_tok[:, :, cols], x[:, cols].rearrange("(t p) c -> p t c", p=P)
                             ).then_inc(x_in[q % XS], 16)

            for n in range(PRO):
                if n >= RING:
                    sp.wait_ge(s_lo, n - AHEAD)
                if n == 0:
                    x_piece(0)
                first_loads(n)
                for q in range(1, XP):
                    if q == n + XA or n == 0 and q < XA:
                        x_piece(q)

            with sp.Fori(0, NKV) as g:
                for c in range(CH):
                    with sp.Fori(0, GC // RING) as j:
                        for k in range(RING):
                            n = PRO + c * GC + k
                            sp.wait_ge(s_lo, g * TURN + j * RING + (n - AHEAD))
                            r0 = j * (RING * GK * P) + k * GK * P
                            if c == KV:
                                strips = w_in[:, C_KV:C_KV + 4 * WKV].rearrange("r (s c) -> r s c", s=4)
                                for kk in range(GK):
                                    sp.dma_start(
                                        raw[n % RING][:, kk * W:(kk + 1) * W].rearrange(
                                            "p (s c) -> p s c", s=4),
                                        strips[bass.ds(r0 + kk * P, P), :, bass.ds(g * HD, HD)]
                                    ).then_inc(landed[n % RING], 16)
                            else:
                                load(n % RING, rows(w_in, r0, GK, g * W + COLS[c], W), (GK, W))

            with sp.Fori(0, NOUT) as c:
                for half in range(2):
                    with sp.Fori(0, GC // RING // 2) as j:
                        for k in range(RING):
                            n = OUT0 + half * GC // 2 + k
                            sp.wait_ge(s_lo, c * GC + j * RING + (n - AHEAD))
                            r0 = j * (RING * GK * P) + ((1 - half) * WC + k * GK * P)
                            load(n % RING, rows(w_out, r0, GK, c * W, W), (GK, W))

            for i in range(FIN):
                t, c = i // NOUT, STORES[i // NOUT][i % NOUT]
                i = t * NOUT + c
                sp.wait_ge(n_out_p if by_pool(i) else n_out_v, finished(i))
                sp.dma_start(out[t * P:(t + 1) * P, c * W:(c + 1) * W], y[:, t, c * W:(c + 1) * W]
                             ).then_inc(stored, 16)
            sp.wait_ge(stored, 16 * FIN)

        @block.gpsimd
        def _(pool):
            pool.memset(ident[:, :], 0.0).then_inc(s_pool, 1)
            pool.memset(causal[:, :], 0.0).then_inc(s_pool, 1)
            pool.memset(c_neg[:, :, :], 0.0).then_inc(s_pool, 1)
            pool.memset(c_ok[:, :, :], 1.0).then_inc(s_pool, 1)
            pool.memset(fold[:, :], 0.0).then_inc(s_pool, 1)
            pool.wait_ge(s_pool, 5)
            pool.affine_select(out=ident[:, :], in_=ident[:, :], compare_op=ALU.not_equal, fill=1.0,
                               base=0, pattern=[[-1, P]], channel_multiplier=1).then_inc(s_const, 1)
            pool.affine_select(out=causal[:, :], in_=causal[:, :], compare_op=ALU.is_ge, fill=NEG,
                               base=0, pattern=[[-1, P]], channel_multiplier=1).then_inc(s_const, 1)
            for m, fill in ((c_neg, NEG), (c_ok, 0.0)):
                pool.affine_select(out=m[:, :, :], in_=m[:, :, :], compare_op=ALU.is_ge, fill=fill,
                                   base=-(LC - 1), pattern=[[P, TT], [-DC, NC]],
                                   channel_multiplier=1).then_inc(s_const, 1)
            for i in range(2):
                for a in range(P // DC):
                    pool.dma_start(pos_sb[a * DC:(a + 1) * DC, i],
                                   pos[i].rearrange("(h b) d -> b h d", h=2)).then_inc(s_small, 16)
                pool.dma_start(w2_sb[:, i], w2[i]).then_inc(s_small, 16)
            pool.dma_start(conv_rows[:, :], conv_w.rearrange("k (b c) -> (k b) c", c=P)
                           ).then_inc(s_small, 16)
            for i in range(2):
                for part in range(2):
                    pool.memset(as_f32(a_t[:, i, 1, part, :, T - DC:T]), 0.0).then_inc(a_pad, 1)
            for half in range(2):
                pool.wait_ge(s_const, 4 + half)
                pool.affine_select(out=fold[:, :], in_=fold[:, :], compare_op=ALU.not_equal, fill=1.0,
                                   base=-half * (P // 2), pattern=[[-1, P // 2]], channel_multiplier=1
                                   ).then_inc(s_const, 1)

            pool.wait_ge(kc_in, 1)
            pool.wait_ge(vc_in, 1)
            pool.wait_ge(vc_h, 2)
            pool.wait_ge(gates_in, 1)
            pool.wait_ge(taps_in, 1)
            with pool.Fori(0, NKV) as g:
                pool.wait_ge(cv.sem, cv.at(g, 0))
                for dst, src in ((keys[:, 0, 0:CP], kc[:, bass.ds(g, 1), :]),
                                 (keys[:, 1, 0:CP], kc[:, bass.ds(g, 1), :]),
                                 (vc_g[0:3 * TQ, :], vc[0:3 * TQ, bass.ds(g, 1), :])):
                    pool.tensor_copy(dst, src.rearrange("p a n -> p (a n)")).then_inc(group_in.sem, 1)
                pool.tensor_copy(taps_g[:, :, :], taps[:, :, bass.ds(g * 4, 4)]).then_inc(group_in.sem, 1)
                pool.tensor_copy(gates_g[:, :, :], gates[:, :, bass.ds(g * (3 * GQA), 3 * GQA)]
                                 ).then_inc(group_in.sem, 1)

            pool.wait_ge(s_used, OUT0)
            pool.dma_start(gamma[:, :], ln_g.to_broadcast([P, D])).then_inc(norm_in, 16)

            def residual(c0, b):
                pool.dma_start(x_res[b][:, :, :], x[:, bass.ds(c0, W)].rearrange("(t p) c -> p t c", p=P)
                               ).then_inc(res_in[b], 16)

            def times_gamma(c0, t):
                v = y[:, t, bass.ds(c0, W)]
                pool.tensor_tensor(v, v, gamma[:, bass.ds(c0, W)], ALU.mult).then_inc(y_gamma, 1)

            def affine_rows(half):
                cols = slice(half * D // 2, (half + 1) * D // 2)
                for row, n, src in ((0, 2, ln_g), (2, 1, ln_b), (LOW, 1, ln_g), (LOW + 1, 1, ln_b)):
                    pool.dma_start(affine_raw[row:row + n, :], src[:, cols].to_broadcast([n, D // 2])
                                   ).then_inc(affine_raw_in, 16)

            pool.wait_ge(y_sum, 4)
            for b in range(2):
                residual(b * W, b)
            pool.memset(affine_raw[:, :], 0.0).then_inc(affine_zero, 1)
            pool.memset(terms[:, :, :], 0.0).then_inc(affine_zero, 1)
            pool.wait_ge(affine_zero, 2)
            for row in (2, LOW + 1):
                pool.memset(terms[:, :, row:row + 1], 1.0).then_inc(terms_0, 1)
            affine_rows(0)
            pool.wait_ge(affine_lo, 1)
            affine_rows(1)
            pool.wait_ge(norm_in, 16)
            with pool.Fori(1, NOUT // 2) as c2:
                for b in range(2):
                    pool.wait_ge(y_sum, c2 * 4 + (2 * b + 2))
                    residual(c2 * (2 * W) + b * W, b)
                    pool.wait_ge(y_stat, c2 * 4 + (2 * b - 2))
                    for t in range(TT):
                        times_gamma(c2 * (2 * W) + (b - 2) * W, t)
            for c in range(NOUT - 2, NOUT - 1):
                pool.wait_ge(y_stat, 2 * c + 2)
                for t in range(TT):
                    times_gamma(c * W, t)
            for t in range(TT):
                pool.wait_ge(y_stat, 2 * NOUT - 1 + t)
                times_gamma((NOUT - 1) * W, t)
                for k in range(NP):
                    n = t * NP + k + 1
                    pool.wait_ge(scaled, n)
                    pool.wait_ge(offset_in, n)
                    v = y[:, t, FIN_P[k] * W:(FIN_P[k] + 1) * W]
                    pool.tensor_tensor(v, v, offset[:, k, :], ALU.add).then_inc(n_out_p, 1)

        @block.scalar
        def _(act):
            def split(n, g=0, per=TURN):
                s = n % RING
                act.wait_ge(landed[s], landed_at(n, g, per))
                if n >= RING:
                    act.wait_ge(s_used, g * per + (n - AHEAD))
                if is_gate(n):
                    dst, src = (m[s][:, :].rearrange("p (k c) -> p k c", c=P) for m in (w_hi, raw))
                    act.activation(dst[:, :, 0:GW], src[:, :, P - GW:P], ACT.Copy).then_inc(s_hi, 1)
                else:
                    act.activation(w_hi[s][:, :], raw[s][:, :], ACT.Copy).then_inc(s_hi, 1)

            def x_high(q):
                act.wait_ge(xt_ps, q + 1)
                act.activation(xt_hi[:, GK * q:GK * (q + 1), :], bank[4 + q % 4][:, :].rearrange(
                    "p (k t) -> p k t", k=GK), ACT.Copy).then_inc(xt_h, 1)

            def a_high(i):
                for b in range(4):
                    act.wait_ge(a_ps, 4 * i + b + 1)
                    dst, src = a_block(i, 0, b)
                    act.activation(dst, src, ACT.Copy).then_inc(a_h, 1)

            x_high(0)
            for n in range(AHEAD):
                split(n)
            for i in range(PRO):
                if i < XP - 1:
                    x_high(i + 1)
                if i == GC + 4:
                    a_high(0)
                if i == MLP_K + 6:
                    act.wait_ge(hid_ps, 1)
                    act.activation(hid[:, 0].rearrange("p g n -> p (g n)"), bank[1][:, 2 * HD:2 * HD + 64],
                                   ACT.Silu).then_inc(hid_in, 1)
                if i == GATE0 + 2:
                    a_high(1)
                split(i + AHEAD)
            act.wait_ge(s_used, PRO)
            act.activation(gate_t[:, :], bank[0][:, 0:T], ACT.Copy).then_inc(gate_t_in, 1)
            act.wait_ge(hid_ps, 2)
            act.activation(hid[:, 1].rearrange("p g n -> p (g n)"), bank[3][:, 0:64],
                           ACT.Silu).then_inc(hid_in, 1)
            act.wait_ge(gate_sum, 1)
            act.activation(gates[:, :, :], gates[:, :, :], ACT.Sigmoid).then_inc(gates_in, 1)
            act.wait_ge(vc_ps, 1)
            act.wait_ge(vc_0, 1)
            for row in (0, 2 * TQ):
                act.activation(vc[row:row + NC, :, :], bank[7][0:NC, :].rearrange("p (g d) -> p g d", g=NKV),
                               ACT.Copy).then_inc(vc_h, 1)

            def evacuate(dst, func, c, g, done):
                act.wait_ge(s_used, chunk_done(g, c))
                for t in range(TT):
                    act.activation(dst[:, t, :], bank[2 * PAIR[c] + t][:, :], func
                                   ).then_inc(done.sem, 1)

            with act.Fori(0, NKV) as g:
                for i in range(TURN):
                    if i == 5:
                        for b in range(2):
                            act.wait_ge(y_in.sem, y_in.at(g, b + 1))
                            act.activation(mix_hi[:, bass.ds(g * 4 + (12 + 2 * b), 2), :],
                                           conv[:, 2 * b:2 * b + 2, :], ACT.Copy).then_inc(y_hi.sem, 1)
                    if i == GC * (ZA + 1):
                        act.wait_ge(cv.sem, cv.at(g, 0))
                        evacuate(tok_a, ACT.Silu, ZA, g, za_tok)
                    if i == GC * (KV + 1):
                        evacuate(tok_b, ACT.Copy, KV, g, kv_tok)
                    if i == GC * (Q + 1):
                        act.wait_ge(z_in.sem, z_in.at(g, 1))
                        evacuate(tok_a, ACT.Copy, Q, g, q_tok)
                    for first, ready, src, dst, done in ((GC * (KV + 1) + 6, k_in, keys, keys_hi, k_hi),
                                                         (GC * (Q + 1) + 6, q_in, q_t, q_hi, q_h)):
                        if i == first:
                            act.wait_ge(ready.sem, ready.at(g, 1))
                            if src is keys:
                                act.wait_ge(group_in.sem, group_in.at(g, 5))
                            act.activation(dst[:, :, :], src[:, :, :], ACT.Copy).then_inc(done.sem, 1)
                            if src is keys:
                                act.activation(v_strips(v_parts, 0, 0), v_strips(tok_b, 0, 1), ACT.Copy
                                               ).then_inc(v_h.sem, 1)
                    for r in range(GQA):
                        if i == I_S + PERIOD * r:
                            act.wait_ge(neg_v.sem, neg_v.at(g, 2 * r + 2))
                            act.activation(ec[:, :, 0:NC], sc[:, :, :], ACT.Exp, scale=SCALE)
                            for t in range(TT):
                                for b in range(2):
                                    last = act.activation(
                                        prob[:, b, t:2 * t + 1, :].rearrange("p k c -> p (k c)"),
                                        scores_of(t, b), ACT.Exp, scale=SCALE, bias=s_neg[:, t, b:b + 1],
                                        accum_out=s_sum[:, t, b + 1:b + 2])
                            last.then_inc(exp_in.sem, 1)
                        if i == I_T + PERIOD * r + NQ:
                            act.wait_ge(pt_in.sem, pt_in.at(g, r + 1))
                            for row in (0, TQ):
                                act.activation(pc_s[row:row + TQ, :], pc_t[2 * TQ:3 * TQ, :], ACT.Copy
                                               ).then_inc(pt_h.sem, 1)
                            act.activation(p_hi[:, :, :, :], p_t[:, :, 0:2, :], ACT.Copy
                                           ).then_inc(pt_h.sem, 1)
                        if i == I_V + PERIOD * r:
                            act.wait_ge(o_in.sem, o_in.at(g, r + 1))
                            act.activation(mix_hi[:, bass.ds(g * 4 + r, 1), :].rearrange("p a t -> p (a t)"),
                                           att[:, :], ACT.Copy).then_inc(o_hi.sem, 1)
                    if i == GC * (H + 1):
                        act.wait_ge(q_in.sem, q_in.at(g, 1))
                        evacuate(tok_a, ACT.Copy, H, g, h_tok)
                    if i == GC * (ZC + 1):
                        evacuate(tok_b, ACT.Silu, ZC, g, zc_tok)
                    split(PRO + i + AHEAD, g)

            for i in range(GC):
                if i == 5:
                    for b in range(2):
                        act.wait_ge(y_in.sem, y_in.at(NKV, b + 1))
                        act.activation(mix_hi[:, KT - 4 + 2 * b:KT - 2 + 2 * b, :],
                                       conv[:, 2 * b:2 * b + 2, :], ACT.Copy).then_inc(y_hi.sem, 1)
                split(OUT0 + i + AHEAD)

            def affine_high(half):
                act.wait_ge(affine_raw_in, 64 * (half + 1))
                act.activation(affine[:, half * D // 2:(half + 1) * D // 2], affine_raw[:, :], ACT.Copy
                               ).then_inc(affine_hi, 1)

            affine_high(0)
            with act.Fori(1, NOUT - 1) as c:
                for i in range(GC):
                    split(OUT0 + i + AHEAD, c, GC)
            affine_high(1)
            for i in range(GC - AHEAD):
                split(OUT0 + (NOUT - 1) * GC + i + AHEAD)

            def deviation(t):
                act.wait_ge(mv_in, t + 1)
                act.activation(std[:, t:t + 1], mv[:, t, 1:2], ACT.Sqrt, bias=eps[:, :]).then_inc(std_in, 1)

            for t in range(TT):
                deviation(t)
                act.wait_ge(terms_ps, t + 1)
                act.activation(terms_t[:, t, :], bank[0][0:RA, 0:P], ACT.Copy).then_inc(terms_t_in, 1)
                for k in range(NP):
                    i = t * NOUT + FIN_P[k]
                    v = y[:, t, FIN_P[k] * W:(FIN_P[k] + 1) * W]
                    if k == 0:
                        act.wait_ge(y_gamma, 2 * NOUT - 2)
                        act.wait_ge(rstd_in, t + 1)
                    act.activation(v, v, ACT.Copy, scale=rstd[:, t:t + 1]).then_inc(scaled, 1)
                    act.wait_ge(offset_ps, i + 1)
                    if t:
                        act.wait_ge(n_out_p, (t - 1) * NP + k + 1)
                    act.activation(offset[:, k, :], bank[2 + i % FB][:, :], ACT.Copy
                                   ).then_inc(offset_in, 1)

        @block.vector
        def _(dve):
            def low(dst, src, high, done):
                dve.tensor_tensor(dst, src, as_f32(high), ALU.subtract).then_inc(done, 1)

            def split(n, g=0, per=TURN, width=GK * W):
                s = n % RING
                dve.wait_ge(s_hi, g * per + (n + 1))
                if is_gate(n):
                    dst, src = (m[s][:, :].rearrange("p (k c) -> p k c", c=P) for m in (w_hi, raw))
                    low(dst[:, :, GW:P], src[:, :, P - GW:P], dst[:, :, 0:GW], s_lo)
                    return
                dve.tensor_tensor(w_lo[s][:, 0:width], raw[s][:, 0:width], as_f32(w_hi[s][:, 0:width]),
                                  ALU.subtract).then_inc(s_lo, 1)

            def x_low(q):
                dve.wait_ge(xt_h, q + 1)
                rows = slice(GK * q, GK * (q + 1))
                low(xt_lo[:, rows, :], bank[4 + q % 4][:, :].rearrange("p (k t) -> p k t", k=GK),
                    xt_hi[:, rows, :], xt_l)

            def a_low(i):
                for b in range(4):
                    dve.wait_ge(a_h, 4 * i + b + 1)
                    dst, src = a_block(i, 1, b)
                    low(dst, src, a_block(i, 0, b)[0], a_l)

            def a_tokens(i):
                for t in range(TT):
                    dve.wait_ge(s_used, (GC, GATE0)[i])
                    for h in range(2):
                        last = dve.tensor_tensor(
                            a_tok[:, i, h, t, :].rearrange("p (g d) -> p g d", g=NKV),
                            bank[2 * i + t][:, :].rearrange("p (g d) -> p g d", g=NKV),
                            pos_sb[:, i, h:h + 1, :].to_broadcast([P, NKV, HD]), ALU.add)
                        last.then_inc(a_in, 1)

            dve.memset(conv[:, :, :], 0.0).then_inc(cv.sem, 1)
            for t in range(TT):
                dve.memset(tok_b[:, t, :], 0.0).then_inc(zc_tok.sem, 1)
            dve.memset(ec[:, :, :], 0.0).then_inc(ec_0, 1)
            dve.memset(as_f32(vc[:, :, :]), 0.0).then_inc(vc_0, 1)
            x_low(0)
            for n in range(AHEAD):
                split(n)
            for i in range(PRO):
                if i < XP - 1:
                    x_low(i + 1)
                if i == GC:
                    dve.wait_ge(s_small, small)
                    a_tokens(0)
                if i == GC + 4:
                    a_low(0)
                if i == GC + 8:
                    dve.wait_ge(taps_ps, 1)
                    dve.tensor_copy(taps[:, :, :].rearrange("p k b -> p (k b)"), bank[6][:, 0:48]
                                    ).then_inc(taps_in, 1)
                if i == MLP_K + 4:
                    dve.wait_ge(s_used, i)
                    dve.tensor_copy(hid_4[:, 0].rearrange("p l e -> p (l e)"), bank[1][:, 0:2 * HD]
                                    ).then_inc(hid_4_in, 1)
                if i == MLP_K + 8:
                    dve.wait_ge(kc_ps, 1)
                    dve.tensor_copy(kc[:, :, :].rearrange("p g n -> p (g n)"), bank[1][:, 384:448]
                                    ).then_inc(kc_in, 1)
                if i == GATE0:
                    a_tokens(1)
                if i == GATE0 + 2:
                    a_low(1)
                if i == MLP_V + 4:
                    dve.wait_ge(s_used, i)
                    dve.tensor_copy(hid_4[:, 1].rearrange("p l e -> p (l e)"), bank[2][:, 0:2 * HD]
                                    ).then_inc(hid_4_in, 1)
                split(i + AHEAD)
            dve.wait_ge(gates_ps, 1)
            logits = bank[1][:, 0:T].rearrange("p (t c) -> p t c", t=TT)
            dve.tensor_copy(gates[:, :, :], logits[:, :, GW - NG:GW]).then_inc(gate_sum_1, 1)
            dve.wait_ge(gate_sum_1, 1)
            dve.tensor_tensor(gates[:, :, :], logits[:, :, P - NG:P], gates[:, :, :], ALU.add
                              ).then_inc(gate_sum, 1)
            dve.wait_ge(vc_h, 2)
            src = bank[7][0:NC, :].rearrange("p (g d) -> p g d", g=NKV)
            low(vc[TQ:TQ + NC, :, :], src, vc[0:NC, :, :], vc_in)

            def gate(g):
                dve.wait_ge(s_used, chunk_done(g, -1))
                dve.wait_ge(zc_tok.sem, zc_tok.at(g, 0))
                for t in range(TT):
                    dve.tensor_tensor(tok_b[:, t, :], bank[4 + t][:, :], tok_b[:, t, :], ALU.mult
                                      ).then_inc(g_tok.sem, 1)

            def quarter(a):
                return slice(TQ * a, TQ * (a + 1))

            def features(dst, src, a):
                for c in range(NQ):
                    last = dve.transpose(
                        dst[quarter(c)].rearrange("p f (t n) -> p t f n", t=TT)[:, :, :, quarter(a)],
                        src[quarter(a)][:, :, :, quarter(c)])
                return last

            def blocks_of(tok):
                return tok[:, :, :].rearrange("p t (f c) -> p t f c", c=P)

            def conv_gate(g, a):
                if a == 0:
                    dve.wait_ge(g_tok.sem, g_tok.at(g, 2))
                last = features(q_t, blocks_of(tok_b), a)
                if a == NQ - 1:
                    last.then_inc(g_in.sem, 1)

            def conv_out(g):
                dve.wait_ge(cv.sem, cv.at(g, 0))
                dve.wait_ge(g_in.sem, g_in.at(g, 1))
                for b in range(2):
                    v = conv[:, 2 * b:2 * b + 2, :]
                    dve.tensor_tensor(v, q_t[:, 2 * b:2 * b + 2, :], v, ALU.mult).then_inc(y_in.sem, 1)

            def conv_low(g, block0):
                for b in range(2):
                    dve.wait_ge(y_hi.sem, y_hi.at(g, b + 1))
                    at = bass.ds(block0 + 2 * b, 2)
                    low(mix_lo[:, at, :], conv[:, 2 * b:2 * b + 2, :], mix_hi[:, at, :], y_lo.sem)

            with dve.Fori(0, NKV) as g:
                for i in range(TURN):
                    if i == 0:
                        gate(g)
                    if 1 <= i <= NQ:
                        conv_gate(g, i - 1)
                    if i == 5:
                        conv_out(g)
                    if i == 6:
                        conv_low(g, g * 4 + 12)
                    for first, ready, src, dst, done in (
                            (GC * (ZA + 1) + 2, za_tok, blocks_of(tok_a), z_t, z_in),
                            (GC * (KV + 1) + 2, kv_tok, blocks_of(tok_b)[:, :, 0:4:2, :],
                             keys[:, :, CP:], k_in),
                            (GC * (Q + 1) + 2, q_tok, blocks_of(tok_a), q_t, q_in)):
                        if i == first:
                            dve.wait_ge(ready.sem, ready.at(g, 2))
                        if first <= i < first + NQ:
                            last = features(dst, src, i - first)
                        if i == first + NQ - 1:
                            last.then_inc(done.sem, 1)
                    for first, high, dst, src, part, done in (
                            (GC * (KV + 1) + 7, k_hi, keys_lo, keys, keys_hi, k_lo),
                            (GC * (Q + 1) + 7, q_h, q_lo, q_t, q_hi, q_l)):
                        if i == first:
                            dve.wait_ge(high.sem, high.at(g, 1))
                            low(dst[:, :, :], src[:, :, :], part[:, :, :], done.sem)
                            if src is keys:
                                dve.wait_ge(v_h.sem, v_h.at(g, 1))
                                low(v_strips(v_parts, 1, 0), v_strips(tok_b, 0, 1),
                                    v_strips(v_parts, 0, 0), v_l.sem)
                    for r in range(GQA):
                        if i == I_S + PERIOD * r:
                            diagonal = causal[:, :].rearrange("p (a k) -> p a k", a=1).to_broadcast([P, 2, P])
                            both = bank[4][:, 0:2 * (CP + P)].rearrange("p (b k) -> p b k", b=2)[:, :, CP:]
                            dve.wait_ge(s_ps.sem, s_ps.at(g, 2 * r + 1))
                            dve.tensor_tensor(both, both, diagonal, ALU.add).then_inc(mask_v.sem, 1)
                            dve.tensor_tensor(sc[:, 0, :], bank[4][:, 0:NC], c_neg[:, 0, :], ALU.add
                                              ).then_inc(mask_v.sem, 1)
                            dve.wait_ge(s_ps.sem, s_ps.at(g, 2 * r + 2))
                            for b in range(2):
                                v = scores_of(1, b)[:, P:T]
                                dve.tensor_tensor(v, v, causal[:, :], ALU.add).then_inc(mask_v.sem, 1)
                            dve.tensor_tensor(sc[:, 1, :], bank[5][:, 0:NC], c_neg[:, 1, :], ALU.add
                                              ).then_inc(mask_v.sem, 1)
                            dve.wait_ge(mask_v.sem, mask_v.at(g, 5 * r + 1))
                            dve.tensor_reduce(s_max[:, 0, :], both, AX.X, ALU.max).then_inc(mx_v.sem, 1)
                            dve.wait_ge(mask_v.sem, mask_v.at(g, 5 * r + 4))
                            for b in range(2):
                                dve.tensor_reduce(s_max[:, 1, b:b + 1], scores_of(1, b), AX.X, ALU.max
                                                  ).then_inc(mx_v.sem, 1)
                            dve.wait_ge(mask_v.sem, mask_v.at(g, 5 * r + 5))
                            dve.tensor_reduce(c_max[:, :], sc[:, :, :], AX.X, ALU.max).then_inc(mx_v.sem, 1)
                            dve.wait_ge(mx_v.sem, mx_v.at(g, 4 * r + 3))
                            dve.tensor_scalar(s_neg[:, :, :], s_max[:, :, :], -SCALE, None, ALU.mult
                                              ).then_inc(neg_v.sem, 1)
                            dve.wait_ge(mx_v.sem, mx_v.at(g, 4 * r + 4))
                            dve.tensor_tensor(sc[:, :, :], sc[:, :, :], c_max[:, :].rearrange(
                                "p (t a) -> p t a", a=1).to_broadcast([P, TT, NC]), ALU.subtract
                                ).then_inc(neg_v.sem, 1)
                        if i == I_S + PERIOD * r + 2:
                            dve.wait_ge(exp_in.sem, exp_in.at(g, r + 1))
                            dve.tensor_reduce(s_sum[:, :, 0], ec[:, :, 0:NC], AX.X, ALU.add
                                              ).then_inc(rcp_v.sem, 1)
                            dve.wait_ge(rcp_v.sem, rcp_v.at(g, 3 * r + 1))
                            dve.reciprocal(s_rcp[:, :, :], s_sum[:, :, :]).then_inc(rcp_v.sem, 1)
                            dve.wait_ge(rcp_v.sem, rcp_v.at(g, 3 * r + 2))
                            dve.tensor_tensor(s_fac[:, :, :], s_rcp[:, :, :],
                                              gates_g[:, :, 3 * r:3 * r + 3], ALU.mult
                                              ).then_inc(rcp_v.sem, 1)
                            dve.wait_ge(rcp_v.sem, rcp_v.at(g, 3 * r + 3))
                            for t in range(TT):
                                v = ec[:, t, 0:NC]
                                dve.scalar_tensor_tensor(out=v, in0=v, scalar=s_fac[:, t, 0:1],
                                                         in1=c_ok[:, t, :], op0=ALU.mult, op1=ALU.mult)
                                for b in range(2):
                                    v = prob[:, b, t:2 * t + 1, :]
                                    last = dve.tensor_scalar(v, v, s_fac[:, t, b + 1:b + 2], None, ALU.mult)
                                last.then_inc(p_in.sem, 1)
                        a = i - (I_T + PERIOD * r)
                        if a == 0:
                            dve.wait_ge(ec_0, 1)
                            dve.wait_ge(p_in.sem, p_in.at(g, 2 * r + 2))
                        if 0 <= a < NQ:
                            dve.transpose(pc_t[2 * TQ:3 * TQ].rearrange("p (t n) -> p t n", t=TT)[:, :, quarter(a)],
                                          ec[quarter(a)])
                            for c in range(NQ):
                                last = dve.transpose(
                                    p_t[quarter(c)].rearrange("p b k n -> p (b k) n")[:, :, quarter(a)],
                                    prob[quarter(a)].rearrange("p b k n -> p (b k) n")[:, :, quarter(c)])
                        if a == NQ - 1:
                            last.then_inc(pt_in.sem, 1)
                        if i == I_T + PERIOD * r + NQ:
                            rows = slice(2 * TQ, 3 * TQ)
                            dve.wait_ge(pt_h.sem, pt_h.at(g, 3 * r + 2))
                            low(pc_s[rows, :], pc_t[rows, :], pc_s[0:TQ, :], pt_l.sem)
                            dve.wait_ge(pt_h.sem, pt_h.at(g, 3 * r + 3))
                            low(p_lo[:, :, 0:2, :], p_t[:, :, 0:2, :], p_hi[:, :, :, :], pt_l.sem)
                        if i == I_V + PERIOD * r:
                            dve.wait_ge(o_ps.sem, o_ps.at(g, r + 1))
                            dve.wait_ge(z_in.sem, z_in.at(g, 1))
                            dve.tensor_tensor(att[:, :], bank[6][:, 0:T], z_t[:, r, :], ALU.mult
                                              ).then_inc(o_in.sem, 1)
                        if i == I_V + PERIOD * r + 1:
                            dve.wait_ge(o_hi.sem, o_hi.at(g, r + 1))
                            at = bass.ds(g * 4 + r, 1)
                            low(mix_lo[:, at, :].rearrange("p a t -> p (a t)"), att[:, :],
                                mix_hi[:, at, :].rearrange("p a t -> p (a t)"), o_lo.sem)
                    if i == GC * (CG + 1):
                        dve.wait_ge(s_used, chunk_done(g, CG))
                        dve.wait_ge(h_tok.sem, h_tok.at(g, 2))
                        for t in range(TT):
                            dve.tensor_tensor(tok_a[:, t, :], bank[2 * PAIR[CG] + t][:, :], tok_a[:, t, :],
                                              ALU.mult).then_inc(u_tok.sem, 1)
                    if i == I_U:
                        dve.wait_ge(u_tok.sem, u_tok.at(g, 2))
                    if I_U <= i < I_U + NQ:
                        last = features(z_t, blocks_of(tok_a), i - I_U)
                    if i == I_U + NQ - 1:
                        last.then_inc(u_in.sem, 1)
                    tap = i - (I_U + NQ)
                    if 0 <= tap < 3:
                        if tap == 0:
                            dve.wait_ge(group_in.sem, group_in.at(g, 5))
                            dve.wait_ge(u_in.sem, u_in.at(g, 1))
                        for f in range(4):
                            w = taps_g[:, 2 - tap, f:f + 1]
                            c = conv[:, f, tap:T]
                            if tap == 0:
                                dve.tensor_scalar(c, z_t[:, f, :], w, None, ALU.mult).then_inc(cv.sem, 1)
                            else:
                                dve.wait_ge(cv.sem, cv.at(g, 4 * tap + f - 3))
                                dve.scalar_tensor_tensor(out=c, in0=z_t[:, f, 0:T - tap], scalar=w, in1=c,
                                                         op0=ALU.mult, op1=ALU.add).then_inc(cv.sem, 1)
                    split(PRO + i + AHEAD, g)

            def tile_sums(c, b, t):
                dve.scalar_tensor_tensor(out=y[:, t, bass.ds(c * W, W)], in0=x_res[b][:, t, :],
                                         scalar=ALPHA, in1=bank[2 * (1 - b) + t][:, :],
                                         op0=ALU.mult, op1=ALU.add).then_inc(y_sum, 1)

            def tile_stats(c, t, sums):
                dve.wait_ge(y_sum, sums)
                st = stats[:, t, bass.ds(c, 1), :].rearrange("p a s -> p (a s)")
                dve.bn_stats(st, y[:, t, bass.ds(c * W, W)]).then_inc(y_stat, 1)

            def chunk_sums(c, b, loads, done, before):
                dve.wait_ge(s_used, done)
                dve.wait_ge(res_in[b], loads)
                for t in range(TT):
                    tile_sums(c, b, t)
                for t in range(TT):
                    tile_stats(c, t, before + (t + 1))

            for i in range(GC):
                if i == 0:
                    gate(NKV)
                if 1 <= i <= NQ:
                    conv_gate(NKV, i - 1)
                if i == 5:
                    conv_out(NKV)
                if i == 6:
                    conv_low(NKV, KT - 4)
                    dve.wait_ge(y_lo.sem, y_lo.at(NKV, 2))
                    dve.memset(eps[:, :], EPS).then_inc(y_sum, 4)
                split(OUT0 + i + AHEAD)

            def affine_low(half):
                v = affine[LOW:RA, half * D // 2:(half + 1) * D // 2]
                dve.wait_ge(affine_hi, half + 1)
                low(v, affine_raw[LOW:RA, :], v, affine_lo)

            affine_low(0)
            with dve.Fori(0, NOUT // 2 - 1) as c2:
                for b in range(2):
                    chunk_sums(c2 * 2 + b, b, c2 * 16 + 16, c2 * (2 * GC) + (OUT0 + (b + 1) * GC),
                               c2 * 4 + (4 + 2 * b))
                    for i in range(GC):
                        split(OUT0 + (b + 1) * GC + i + AHEAD, c2, 2 * GC)
            c = NOUT - 2
            chunk_sums(c, 0, c // 2 * 16 + 16, OUT0 + (c + 1) * GC, 4 + 2 * c)
            affine_low(1)
            for i in range(GC - AHEAD):
                split(OUT0 + (NOUT - 1) * GC + i + AHEAD)

            def mean_var(t):
                tile_sums(NOUT - 1, 1, t)
                tile_stats(NOUT - 1, t, 4 + 2 * (NOUT - 1) + t + 1)
                dve.wait_ge(y_stat, 2 * NOUT - 1 + t)
                dve.bn_aggr(mv[:, t, :], stats[:, t, :, :].rearrange("p c s -> p (c s)")
                            ).then_inc(mv_in, 1)

            def scale_shift(t):
                dve.wait_ge(std_in, t + 1)
                dve.reciprocal(rstd[:, t:t + 1], std[:, t:t + 1]).then_inc(rstd_in, 1)
                dve.wait_ge(rstd_in, t + 1)
                for dst, n in ((shift[:, t:t + 1], 1), (terms[:, t, 0:RA:LOW].bitcast(F32R), 2)):
                    dve.scalar_tensor_tensor(out=dst, in0=mv[:, t, 0:1].to_broadcast([P, n]), scalar=-1.0,
                                             in1=rstd[:, t:t + 1].to_broadcast([P, n]),
                                             op0=ALU.mult, op1=ALU.mult).then_inc(shift_in, 1)
                dve.wait_ge(shift_in, 2 * t + 2)
                dve.tensor_tensor(terms[:, t, 1:2], shift[:, t:t + 1], terms[:, t, 0:1], ALU.subtract
                                  ).then_inc(terms_in, 1)

            def finish(i):
                t, c = divmod(i, NOUT)
                v = y[:, t, c * W:(c + 1) * W]
                dve.wait_ge(y_gamma, 2 * NOUT - 2 if c < NOUT - 1 else 2 * NOUT - 1 + t)
                dve.wait_ge(offset_ps, i + 1)
                dve.scalar_tensor_tensor(out=v, in0=v, scalar=rstd[:, t:t + 1], in1=bank[2 + i % FB][:, :],
                                         op0=ALU.mult, op1=ALU.add).then_inc(n_out_v, 1)

            dve.wait_ge(terms_0, 2)
            dve.wait_ge(out_tile0, 1)
            dve.wait_ge(res_in[1], NOUT // 2 * 16)
            mean_var(0)
            scale_shift(0)
            rest = [i for i in range(FIN) if not by_pool(i)]
            for i in rest[:NV - 2]:
                finish(i)
            dve.wait_ge(s_used, LAST)
            mean_var(1)
            scale_shift(1)
            for i in rest[NV - 2:]:
                finish(i)

        @block.tensor
        def _(pe):
            def granule(n, hi, lo, k0, pair, first, last, rows=range(GK), tokens=range(TT)):
                s = n % RING
                for k in rows:
                    wh, wl = w_hi[s][:, k * W:(k + 1) * W], w_lo[s][:, k * W:(k + 1) * W]
                    for t in tokens:
                        xh, xl = (m[:, k0 + k, t * P:(t + 1) * P] for m in (hi, lo))
                        acc = bank[2 * pair + t][:, :]
                        pe.matmul(acc, xh, wl, start=first and k == 0, stop=False)
                        pe.matmul(acc, xh, wh, start=False, stop=False)
                        mm = pe.matmul(acc, xl, wh, start=False, stop=last and k == GK - 1)
                return mm

            def transpose(dst, src):
                rows = src.shape[0]
                return pe.transpose(dst, src, ident[0:rows, 0:rows])

            def x_transposes(q):
                pe.wait_ge(x_in[q % XS], 16 * (q // XS + 1))
                if q >= 4:
                    pe.wait_ge(xt_l, q - 3)
                for k in range(GK):
                    for t in range(TT):
                        kt = GK * q + k
                        last = transpose(bank[4 + q % 4][:, k * T + t * P:k * T + (t + 1) * P],
                                         x_tok[:, t, kt * P:(kt + 1) * P])
                last.then_inc(xt_ps, 1)

            def a_transposes(i):
                pe.wait_ge(a_in, 4 * i + 4)
                for b in range(4):
                    if i == 0:
                        pe.wait_ge(xt_l, XP)
                    else:
                        pe.wait_ge(taps_in, 1)
                    h = b // 2
                    for gg in range(2):
                        g = b % 2 * 2 + gg
                        for t in range(TT):
                            last = transpose(bank[4 + b][:, gg * T + t * P:gg * T + (t + 1) * P],
                                             a_tok[:, i, h, t, g * HD:(g + 1) * HD])
                    last.then_inc(a_ps, 1)

            def chunk_granules(base, g, per, hi, lo, pair, steps):
                for j in range(GC):
                    steps(j)
                    n = base + j
                    if base == GC and n >= MLP_K:
                        n += 4
                    pe.wait_ge(s_lo, g * per + (n + 1))
                    granule(n, hi, lo, GK * j, pair, j == 0, j == GC - 1).then_inc(s_used, 1)

            pe.wait_ge(s_const, 1)
            x_transposes(0)

            def chunk0_steps(j):
                if j < XP - 1:
                    x_transposes(j + 1)
                pe.wait_ge(xt_l, j + 1)

            def mlp(i, j, acc):
                n = (MLP_K, MLP_V)[i] + j
                pe.wait_ge(s_lo, n + 1)
                pe.wait_ge(a_l, 4 * i + 4)
                for k in range(8):
                    h, at = divmod(8 * j + k, DC)
                    tokens = a_t[:, i, h].rearrange("p l g t -> p l (g t)")[:, :, at:NKV * T:DC]
                    mm = pe.matmul(acc.rearrange("p (l e) -> p l e", l=2), tokens,
                                   parts[n % RING][:, :, k * HD:(k + 1) * HD],
                                   start=j == 0 and k == 0, stop=j == 3 and k == 7)
                mm.then_inc(s_used, 1)

            def sum_parts(i, acc):
                pe.wait_ge(hid_4_in, i + 1)
                pe.matmul(acc, hid_4[:, i, 0, :], fold[:, :], start=True, stop=False)
                pe.matmul(acc, hid_4[:, i, 1, :], fold[:, :], start=False, stop=True).then_inc(hid_ps, 1)

            def chunk1_steps(j):
                i = GC + j + (4 if j >= MLP_K - GC else 0)
                if i == GC + 4:
                    a_transposes(0)
                if i == GC + 8:
                    pe.wait_ge(s_small, small)
                    pe.wait_ge(a_l, 4)
                    transpose(bank[6][:, 0:48], conv_rows[:, :]).then_inc(taps_ps, 1)
                if i == MLP_K + 4:
                    pe.wait_ge(a_pad, 4)
                    for m in range(4):
                        mlp(0, m, bank[1][:, 0:2 * HD])
                if i == MLP_K + 6:
                    pe.wait_ge(s_const, 6)
                    sum_parts(0, bank[1][:, 2 * HD:2 * HD + 64])
                if i == MLP_K + 8:
                    pe.wait_ge(hid_in, 1)
                    pe.matmul(bank[1][:, 384:448], w2_sb[:, 0, :], hid[:, 0].rearrange("p g n -> p (g n)"),
                              start=True, stop=True).then_inc(kc_ps, 1)

            def gate_granule(n):
                pe.wait_ge(s_lo, n + 1)
                j = n - GATE0 - (4 if n >= MLP_V else 0)
                for k in range(8):
                    for m in (xt_lo, xt_hi):
                        mm = pe.matmul(bank[0][:, 0:T], w_hi[n % RING][:, k * P:(k + 1) * P], m[:, 8 * j + k, :],
                                       start=j == 0 and k == 0 and m is xt_lo,
                                       stop=j == 3 and k == 7 and m is xt_hi)
                mm.then_inc(s_used, 1)

            chunk_granules(0, 0, 0, xt_hi, xt_lo, 0, chunk0_steps)
            chunk_granules(GC, 0, 0, xt_hi, xt_lo, 1, chunk1_steps)
            gate_granule(GATE0)
            a_transposes(1)
            gate_granule(GATE0 + 1)
            gate_granule(GATE0 + 2)
            for m in range(4):
                mlp(1, m, bank[2][:, 0:2 * HD])
            gate_granule(MLP_V + 4)
            sum_parts(1, bank[3][:, 0:64])
            pe.wait_ge(gate_t_in, 1)
            for t in range(TT):
                last = transpose(bank[1][:, t * P:(t + 1) * P], gate_t[:, t * P:(t + 1) * P])
            last.then_inc(gates_ps, 1)
            pe.wait_ge(hid_in, 2)
            for g in range(NKV):
                mm = pe.matmul(bank[7][0:NC, g * HD:(g + 1) * HD], hid[:, 1, g, 0:NC], w2_sb[:, 1, :],
                               start=True, stop=True)
            mm.then_inc(vc_ps, 1)

            def group_steps(g, i):
                if i == 0:
                    pe.wait_ge(cv.sem, cv.at(g, 0))
                if i == GC * KV:
                    pe.wait_ge(gates_in, 1)
                    pe.wait_ge(zc_tok.sem, zc_tok.at(g, 0))
                if i == GC * Q:
                    pe.wait_ge(za_tok.sem, za_tok.at(g, 2))
                if i == GC * H:
                    pe.wait_ge(kv_tok.sem, kv_tok.at(g, 2))
                if i == GC * CG:
                    pe.wait_ge(q_tok.sem, q_tok.at(g, 2))
                for r in range(GQA):
                    if i == I_S + PERIOD * r:
                        if r:
                            pe.wait_ge(exp_in.sem, exp_in.at(g, r))
                        else:
                            pe.wait_ge(vc_in, 1)
                            pe.wait_ge(vc_h, 2)
                            pe.wait_ge(g_tok.sem, g_tok.at(g, 2))
                            pe.wait_ge(k_lo.sem, k_lo.at(g, 1))
                            pe.wait_ge(q_l.sem, q_l.at(g, 1))
                        first = bank[4][:, 0:2 * (CP + P)].rearrange("p (b k) -> p b k", b=2)
                        for t, acc, at in ((0, first, (slice(0, 2), slice(0, CP + P))),
                                           (1, bank[5][:, 0:CP + T], (0, slice(0, CP + T))),
                                           (1, bank[7][:, 0:T], (1, slice(CP, CP + T)))):
                            qh, ql = (m[:, r, t * P:(t + 1) * P] for m in (q_hi, q_lo))
                            kh, kl = (m[(slice(0, P),) + at] for m in (keys_hi, keys_lo))
                            pe.matmul(acc, qh, kl, start=True, stop=False)
                            pe.matmul(acc, qh, kh, start=False, stop=False)
                            mm = pe.matmul(acc, ql, kh, start=False, stop=True)
                            if at[0] != 0:
                                mm.then_inc(s_ps.sem, 1)
                    if i == I_V + PERIOD * r:
                        pe.wait_ge(pt_in.sem, pt_in.at(g, r + 1))
                        pe.wait_ge(pt_l.sem, pt_l.at(g, 2 * r + 2))
                        pe.wait_ge(v_l.sem, v_l.at(g, 1))
                        if r:
                            pe.wait_ge(o_in.sem, o_in.at(g, r))
                        acc = bank[6][:, 0:T]
                        pe.matmul(acc, vc_g[0:3 * TQ, :], pc_s[0:3 * TQ, :], start=True, stop=False)
                        for b in range(2):
                            vh, vl = (v_strips(v_parts, m, 0)[:, b, :] for m in range(2))
                            ph, pl = (m[:, b, 0:2, :].rearrange("p k n -> p (k n)") for m in (p_hi, p_lo))
                            pe.matmul(acc, vh, pl, start=False, stop=False)
                            pe.matmul(acc, vh, ph, start=False, stop=False)
                            pe.matmul(acc, vl, ph, start=False, stop=False)
                            mm = pe.matmul(acc[:, P:T], v_strips(tok_b, 1, 1)[:, b, :], p_t[:, b, 2, :],
                                           start=False, stop=b == 1)
                        mm.then_inc(o_ps.sem, 1)
                if i == GC * ZC:
                    pe.wait_ge(h_tok.sem, h_tok.at(g, 2))
                if i == GC * BG:
                    pe.wait_ge(exp_in.sem, exp_in.at(g, GQA))

            with pe.Fori(0, NKV) as g:
                for c in range(CH):
                    chunk_granules(PRO + c * GC, g, TURN, xt_hi, xt_lo, PAIR[c],
                                   lambda j, c=c: group_steps(g, c * GC + j))

            def first_steps(j):
                if j == 0:
                    pe.wait_ge(cv.sem, cv.at(NKV, 0))
                if j == 14:
                    pe.wait_ge(y_lo.sem, y_lo.at(NKV, 2))

            def second_steps(j):
                if j == 0:
                    pe.wait_ge(zc_tok.sem, zc_tok.at(NKV, 0))

            def no_steps(j):
                pass

            chunk_granules(OUT0, 0, 2 * GC, mix_hi, mix_lo, 1, first_steps)
            chunk_granules(OUT0 + GC, 0, 2 * GC, mix_hi, mix_lo, 0, second_steps)
            with pe.Fori(1, NOUT // 2 - 1) as c2:
                for b in range(2):
                    pe.wait_ge(y_sum, c2 * 4 + (2 * b + 2))
                    chunk_granules(OUT0 + b * GC, c2, 2 * GC, mix_hi, mix_lo, 1 - b, no_steps)
            pe.wait_ge(y_sum, 2 * NOUT - 2)
            chunk_granules(LAST - 2 * GC, 0, 0, mix_hi, mix_lo, 1, no_steps)
            pe.wait_ge(y_sum, 2 * NOUT)
            for j in range(GC - RING):
                n = LAST - GC + j
                pe.wait_ge(s_lo, n + 1)
                granule(n, mix_hi, mix_lo, GK * j, 0, j == 0, False).then_inc(s_used, 1)

            def last_granule(j, rows, t):
                return granule(LAST - GC + j, mix_hi, mix_lo, GK * j, 0, False, j == GC - 1, rows, (t,))

            def terms_transpose(t):
                pe.wait_ge(terms_in, t + 1)
                if t:
                    pe.wait_ge(terms_t_in, t)
                transpose(bank[0][0:RA, 0:P], terms[:, t, :]).then_inc(terms_ps, 1)

            def offsets(blocks):
                for i in blocks:
                    t, c = divmod(i, NOUT)
                    if i >= FB:
                        if by_pool(i - FB):
                            pe.wait_ge(offset_in, finished(i - FB))
                        else:
                            pe.wait_ge(n_out_v, finished(i - FB))
                    pe.matmul(bank[2 + i % FB][:, :], terms_t[:, t, :], affine[:, c * W:(c + 1) * W],
                              start=True, stop=True).then_inc(offset_ps, 1)

            for j in range(GC - RING, GC):
                pe.wait_ge(s_lo, LAST - GC + j + 1)
                mm = last_granule(j, range(GK), 0)
            mm.then_inc(out_tile0, 1)
            for j in range(GC - RING, GC):
                for k in range(GK):
                    row = GK * j + k - KT
                    if row == -4:
                        terms_transpose(0)
                    if row == -3:
                        pe.wait_ge(terms_t_in, 1)
                        pe.wait_ge(affine_lo, 2)
                        offsets(range(2))
                    if row >= -2:
                        offsets((row + 4,))
                    mm = last_granule(j, (k,), 1)
                mm.then_inc(s_used, 1)
            offsets(range(4, NOUT))
            terms_transpose(1)
            pe.wait_ge(terms_t_in, 2)
            offsets(range(NOUT, FIN))


NAMES = ["x", "w_in", "conv_w", "cmp_pos_k", "cmp_w1_k", "cmp_w2_k", "cmp_pos_v", "cmp_w1_v",
         "cmp_w2_v", "w_out", "ln_g", "ln_b"]


def kernel(**inputs):
    import concourse.bacc as bacc
    from concourse.bass_utils import run_bass_kernel_spmd as run

    nc = bacc.Bacc("TRN2", target_bir_lowering=False, num_devices=1, dynamic_dma_scratch_size=8192)
    arrays, args = {}, []
    for name in NAMES:
        a = np.ascontiguousarray(inputs[name])
        arrays[f"in_{name}"] = a
        args.append(nc.dram_tensor(f"in_{name}", a.shape, mybir.dt.from_np(a.dtype),
                                   kind="ExternalInput").ap())
    o = nc.dram_tensor("out_y", (1, T, D), F32, kind="ExternalOutput").ap()
    build(nc, *args, o)
    return run(nc, [arrays], core_ids=[0]).results[0]["out_y"]
```
